# Optimizing a Trainium2 kernel written in Bass

```python
import math
import jax, jax.numpy as jnp
from jax import lax
import numpy as np

D_MODEL = 1024
BATCH = 1
SEQ = 1024
DEPTH = 1

HEAD_DIM = 64
NSA_HEADS = 8
NSA_KV_HEADS = 2
NSA_GROUP = NSA_HEADS // NSA_KV_HEADS
SB_HEADS = 8
NSA_WIDTH = NSA_HEADS * HEAD_DIM
SB_WIDTH = SB_HEADS * HEAD_DIM
MIX_WIDTH = NSA_WIDTH + SB_WIDTH
NSA_KV_WIDTH = NSA_KV_HEADS * HEAD_DIM
N_BRANCH = 3
CMP_LEN = 32
CMP_STRIDE = 16
CMP_HIDDEN = HEAD_DIM
SLC_LEN = 64
SLC_TOPN = 16
WINDOW = 512
Q_BLOCK = 128
ROPE_DIM = HEAD_DIM // 4
ROPE_THETA = 500000.0
EPS = 1e-6
FORCE_BONUS = 1.0e4
IN_SIZES = (NSA_WIDTH,
            NSA_KV_WIDTH, NSA_KV_WIDTH,
            NSA_KV_WIDTH, NSA_KV_WIDTH,
            NSA_KV_WIDTH, NSA_KV_WIDTH,
            NSA_HEADS * N_BRANCH,
            NSA_WIDTH,
            SB_WIDTH, SB_WIDTH, SB_WIDTH,
            SB_WIDTH)
IN_COLS = sum(IN_SIZES)

kernel_name = "hybrid_nsa_stickbreaking_layer"

def rms_norm(x, g):
    xf = x.astype(jnp.float32)
    y = xf * lax.rsqrt(jnp.mean(xf * xf, axis=-1, keepdims=True) + EPS)
    return (y * g.astype(jnp.float32)).astype(x.dtype)

def rope_partial(x, pos):
    inv_freq = jnp.power(ROPE_THETA, -jnp.arange(0, ROPE_DIM, 2, dtype=jnp.float32) / ROPE_DIM)
    ang = pos.astype(jnp.float32)[:, None] * inv_freq[None, :]
    cos = jnp.cos(ang).astype(x.dtype)
    sin = jnp.sin(ang).astype(x.dtype)
    half = ROPE_DIM // 2
    x1, x2, rest = x[..., :half], x[..., half:ROPE_DIM], x[..., ROPE_DIM:]
    return jnp.concatenate([x1 * cos - x2 * sin, x2 * cos + x1 * sin, rest], axis=-1)

def masked_softmax(logits, mask):
    logits = jnp.where(mask, logits.astype(jnp.float32), -jnp.inf)
    m = jnp.max(logits, axis=-1, keepdims=True)
    m = jnp.where(jnp.isfinite(m), m, 0.0)
    p = jnp.where(mask, jnp.exp(logits - m), 0.0)
    return p / jnp.maximum(jnp.sum(p, axis=-1, keepdims=True), 1e-30)

def compress(blocks, pos_emb, w1, b1, w2):
    b_, g_, n_, l_, d_ = blocks.shape
    flat = (blocks + pos_emb).reshape(b_, g_, n_, l_ * d_)
    return jax.nn.silu(flat @ w1 + b1) @ w2

def setup_inputs(seed: int = 0) -> dict:
    key = jax.random.key(seed)
    ks = jax.random.split(key, 20)
    f32 = jnp.float32
    nrm = lambda k, shape, s: jax.random.normal(k, shape, f32) * s
    return {
        "x": nrm(ks[0], (BATCH, SEQ, D_MODEL), 1.0),
        "norm_gain": 1.0 + nrm(ks[1], (D_MODEL,), 0.01),
        "w_in": nrm(ks[2], (D_MODEL, IN_COLS), D_MODEL ** -0.5),
        "q_norm_gain": 1.0 + nrm(ks[3], (HEAD_DIM,), 0.01),
        "k_norm_cmp": 1.0 + nrm(ks[4], (HEAD_DIM,), 0.01),
        "k_norm_slc": 1.0 + nrm(ks[5], (HEAD_DIM,), 0.01),
        "k_norm_win": 1.0 + nrm(ks[6], (HEAD_DIM,), 0.01),
        "cmp_k_pos": nrm(ks[7], (CMP_LEN, HEAD_DIM), 0.02),
        "cmp_k_w1": nrm(ks[8], (CMP_LEN * HEAD_DIM, CMP_HIDDEN), (CMP_LEN * HEAD_DIM) ** -0.5),
        "cmp_k_b1": nrm(ks[9], (CMP_HIDDEN,), 0.01),
        "cmp_k_w2": nrm(ks[10], (CMP_HIDDEN, HEAD_DIM), CMP_HIDDEN ** -0.5),
        "cmp_v_pos": nrm(ks[11], (CMP_LEN, HEAD_DIM), 0.02),
        "cmp_v_w1": nrm(ks[12], (CMP_LEN * HEAD_DIM, CMP_HIDDEN), (CMP_LEN * HEAD_DIM) ** -0.5),
        "cmp_v_b1": nrm(ks[13], (CMP_HIDDEN,), 0.01),
        "cmp_v_w2": nrm(ks[14], (CMP_HIDDEN, HEAD_DIM), CMP_HIDDEN ** -0.5),
        "w_out": nrm(ks[15], (MIX_WIDTH, D_MODEL), MIX_WIDTH ** -0.5),
    }

def reference(x, norm_gain, w_in, q_norm_gain, k_norm_cmp, k_norm_slc, k_norm_win,
              cmp_k_pos, cmp_k_w1, cmp_k_b1, cmp_k_w2,
              cmp_v_pos, cmp_v_w1, cmp_v_b1, cmp_v_w2, w_out):
    B, S, _ = x.shape
    G, R, D = NSA_KV_HEADS, NSA_GROUP, HEAD_DIM
    nq = S // Q_BLOCK
    scale = 1.0 / math.sqrt(D)
    pos = jnp.arange(S, dtype=jnp.int32)

    def heads(t, n):
        return t.reshape(B, S, n, D).transpose(0, 2, 1, 3)

    for _layer in range(DEPTH):
        h = rms_norm(x, norm_gain)
        proj = h @ w_in
        parts, off = [], 0
        for sz in IN_SIZES:
            parts.append(proj[..., off:off + sz])
            off += sz
        (q_n, kc, vc, ks_, vs_, kw, vw, gate_logits, gate_nsa,
         q_sb, k_sb, v_sb, gate_sb) = parts

        q = rope_partial(rms_norm(heads(q_n, NSA_HEADS), q_norm_gain), pos)
        qg = q.reshape(B, G, R, S, D)

        n_cmp = (S - CMP_LEN) // CMP_STRIDE + 1
        tok_idx = jnp.arange(n_cmp)[:, None] * CMP_STRIDE + jnp.arange(CMP_LEN)[None, :]
        kc_blk = heads(kc, G)[:, :, tok_idx]
        vc_blk = heads(vc, G)[:, :, tok_idx]
        cmp_end = jnp.arange(n_cmp, dtype=jnp.int32) * CMP_STRIDE + (CMP_LEN - 1)
        k_cmp = rope_partial(rms_norm(compress(kc_blk, cmp_k_pos, cmp_k_w1, cmp_k_b1, cmp_k_w2),
                                      k_norm_cmp), cmp_end)
        v_cmp = compress(vc_blk, cmp_v_pos, cmp_v_w1, cmp_v_b1, cmp_v_w2)
        cmp_logits = jnp.einsum('bgrtd,bgnd->bgrtn', qg, k_cmp) * scale
        cmp_mask = cmp_end[None, :] <= pos[:, None]
        p_cmp = masked_softmax(cmp_logits, cmp_mask)
        o_cmp = jnp.einsum('bgrtn,bgnd->bgrtd', p_cmp.astype(v_cmp.dtype), v_cmp)

        n_slc = S // SLC_LEN
        cs = jnp.arange(n_cmp) * CMP_STRIDE
        ss = jnp.arange(n_slc) * SLC_LEN
        overlap = jnp.clip(jnp.minimum(cs[:, None] + CMP_LEN, ss[None, :] + SLC_LEN)
                           - jnp.maximum(cs[:, None], ss[None, :]), 0, None)
        overlap = overlap.astype(jnp.float32) / CMP_LEN
        p_slc = jnp.einsum('bgrtn,nj->bgtj', p_cmp, overlap)
        blk_t = pos // SLC_LEN
        j_idx = jnp.arange(n_slc)
        slc_valid = j_idx[None, :] <= blk_t[:, None]
        forced = (j_idx[None, :] == 0) | (j_idx[None, :] == blk_t[:, None]) | (j_idx[None, :] == blk_t[:, None] - 1)
        sel_logit = jnp.where(slc_valid, p_slc + jnp.where(forced, FORCE_BONUS, 0.0), -jnp.inf)
        top_n = min(SLC_TOPN, n_slc)
        sel_score, sel_idx = lax.top_k(sel_logit, top_n)
        sel_ok = jnp.isfinite(sel_score)

        k_slc = rope_partial(rms_norm(heads(ks_, G), k_norm_slc), pos).reshape(B, G, n_slc, SLC_LEN, D)
        v_slc = heads(vs_, G).reshape(B, G, n_slc, SLC_LEN, D)
        qb = jnp.moveaxis(qg.reshape(B, G, R, nq, Q_BLOCK, D), 3, 0)
        idx_b = jnp.moveaxis(sel_idx.reshape(B, G, nq, Q_BLOCK, top_n), 2, 0)
        ok_b = jnp.moveaxis(sel_ok.reshape(B, G, nq, Q_BLOCK, top_n), 2, 0)
        pos_b = pos.reshape(nq, Q_BLOCK)
        b_ix = jnp.arange(B)[:, None, None, None]
        g_ix = jnp.arange(G)[None, :, None, None]
        n_keys = top_n * SLC_LEN

        def slc_block(args):
            q_i, idx_i, ok_i, t_i = args
            k_sel = k_slc[b_ix, g_ix, idx_i].reshape(B, G, Q_BLOCK, n_keys, D)
            v_sel = v_slc[b_ix, g_ix, idx_i].reshape(B, G, Q_BLOCK, n_keys, D)
            key_pos = (idx_i[..., None] * SLC_LEN + jnp.arange(SLC_LEN)).reshape(B, G, Q_BLOCK, n_keys)
            ok = jnp.repeat(ok_i, SLC_LEN, axis=-1) & (key_pos <= t_i[None, None, :, None])
            logits = jnp.einsum('bgrtd,bgtkd->bgrtk', q_i, k_sel) * scale
            p = masked_softmax(logits, ok[:, :, None])
            return jnp.einsum('bgrtk,bgtkd->bgrtd', p.astype(v_sel.dtype), v_sel)

        o_slc = lax.map(slc_block, (qb, idx_b, ok_b, pos_b))
        o_slc = jnp.moveaxis(o_slc, 0, 3).reshape(B, G, R, S, D)

        n_wb = WINDOW // Q_BLOCK
        k_win = rope_partial(rms_norm(heads(kw, G), k_norm_win), pos)
        v_win = heads(vw, G)
        padw = ((0, 0), (0, 0), (WINDOW, 0), (0, 0))
        kpad = jnp.pad(k_win, padw).reshape(B, G, nq + n_wb, Q_BLOCK, D)
        vpad = jnp.pad(v_win, padw).reshape(B, G, nq + n_wb, Q_BLOCK, D)
        k_band = jnp.concatenate([kpad[:, :, i:i + nq] for i in range(n_wb + 1)], axis=3)
        v_band = jnp.concatenate([vpad[:, :, i:i + nq] for i in range(n_wb + 1)], axis=3)
        band_len = (n_wb + 1) * Q_BLOCK
        kp = jnp.arange(nq)[:, None] * Q_BLOCK - WINDOW + jnp.arange(band_len)[None, :]
        qp = pos.reshape(nq, Q_BLOCK)
        dist = qp[:, :, None] - kp[:, None, :]
        win_mask = (kp[:, None, :] >= 0) & (dist >= 0) & (dist < WINDOW)
        qw = qg.reshape(B, G, R, nq, Q_BLOCK, D)
        w_logits = jnp.einsum('bgrnqd,bgnkd->bgrnqk', qw, k_band) * scale
        p_win = masked_softmax(w_logits, win_mask)
        o_win = jnp.einsum('bgrnqk,bgnkd->bgrnqd', p_win.astype(v_band.dtype), v_band).reshape(B, G, R, S, D)

        gates = jax.nn.sigmoid(gate_logits.reshape(B, S, NSA_HEADS, N_BRANCH).transpose(0, 2, 1, 3)
                               .reshape(B, G, R, S, N_BRANCH))
        o_nsa = gates[..., 0:1] * o_cmp + gates[..., 1:2] * o_slc + gates[..., 2:3] * o_win
        o_nsa = o_nsa.reshape(B, NSA_HEADS, S, D).transpose(0, 2, 1, 3).reshape(B, S, NSA_WIDTH)
        o_nsa = o_nsa * jax.nn.silu(gate_nsa)

        q_s = heads(q_sb, SB_HEADS)
        k_s = heads(k_sb, SB_HEADS)
        v_s = heads(v_sb, SB_HEADS)
        qsb_b = jnp.moveaxis(q_s.reshape(B, SB_HEADS, nq, Q_BLOCK, D), 2, 0)

        def sb_block(args):
            q_i, t_i = args
            z = jnp.einsum('bhtd,bhsd->bhts', q_i, k_s).astype(jnp.float32) * scale
            causal = pos[None, :] < t_i[:, None]
            log_1m = jnp.where(causal, jax.nn.log_sigmoid(-z), 0.0)
            after = lax.cumsum(log_1m, axis=3, reverse=True) - log_1m
            a = jnp.where(causal, jnp.exp(jax.nn.log_sigmoid(z) + after), 0.0)
            return jnp.einsum('bhts,bhsd->bhtd', a.astype(v_s.dtype), v_s)

        o_sb = lax.map(sb_block, (qsb_b, pos_b))
        o_sb = jnp.moveaxis(o_sb, 0, 2).reshape(B, SB_HEADS, S, D).transpose(0, 2, 1, 3).reshape(B, S, SB_WIDTH)
        o_sb = o_sb * jax.nn.silu(gate_sb)

        mix = jnp.concatenate([o_nsa, o_sb], axis=-1)
        x = x + mix @ w_out
    return x


_drawn_inputs = setup_inputs


def setup_inputs(seed=0):
    import zlib

    import numpy as np

    out = dict(_drawn_inputs(seed))
    spreads = {}
    factors = {'norm_gain': 8.0,
     'q_norm_gain': 8.0,
     'k_norm_cmp': 36.12,
     'k_norm_slc': 8.0,
     'k_norm_win': 8.0,
     'cmp_k_pos': 8.0,
     'cmp_k_b1': 29.585,
     'cmp_v_pos': 64.0,
     'cmp_v_b1': 64.0}
    for name, (base, spread) in spreads.items():
        noise = np.random.default_rng([zlib.crc32(name.encode()), seed]).standard_normal(out[name].shape)
        drawn = base * np.exp(spread * noise) if base else spread * noise
        out[name] = __import__('jax').numpy.asarray(drawn.astype(out[name].dtype))
    for name, factor in factors.items():
        out[name] = (out[name] * factor).astype(out[name].dtype)
    return out
```

```python
from contextlib import ExitStack

import numpy as np

import concourse.bass as bass
from concourse import mybir

F32 = mybir.dt.float32
F32R = mybir.dt.float32r
BF16 = mybir.dt.bfloat16
ALU = mybir.AluOpType
ACT = mybir.ActivationFunctionType
AX_X = mybir.AxisListType.X

P = 128
S = 1024
D = 1024
DH = 64
KT = D // P
NT = S // P
HALF = 512
NSA_HEADS, KV_HEADS, SB_HEADS = 8, 2, 8
GROUP = NSA_HEADS // KV_HEADS
HEADS = NSA_HEADS + SB_HEADS
N_BRANCH = 3
CMP_LEN, CMP_STRIDE = 32, 16
N_CMP = (S - CMP_LEN) // CMP_STRIDE + 1
CW = 64
WIN_TILES = 512 // P
ROPE = DH // 4
EPS = 1e-6
SCALE = 1.0 / 8.0
MASK = -1e30
NEG_MAX_CAP = 1e29

C_Q, C_KC, C_VC, C_KS, C_VS, C_KW, C_VW = 0, 512, 640, 768, 896, 1024, 1152
C_GL, C_GN, C_QB, C_KB, C_VB, C_GB = 1280, 1304, 1816, 2328, 2840, 3352
TILES = [("norm", 0, C_KS, P), ("val", 0, C_VS, P), ("norm", 1, C_KW, P), ("val", 1, C_VW, P)]
for _i in range(4):
    TILES += [("norm", 2 + _i, C_Q + P * _i, P), ("gate", _i, C_GN + P * _i, P)]
TILES += [("logit", 0, C_GL, NSA_HEADS * N_BRANCH), ("cmp", 0, C_KC, P)]
for _i in range(4):
    TILES += [("cmp", 1, C_VC, P)] if _i == 1 else []
    TILES += [("sbq", _i, C_QB + P * _i, P), ("sbk", _i, C_KB + P * _i, P),
              ("val", 2 + _i, C_VB + P * _i, P), ("gate", 4 + _i, C_GB + P * _i, P)]
N_IN = len(TILES)
N_OUT = D // P
HL = [(k, i) for k, i, _, _ in TILES if k in ("norm", "sbq", "sbk")]
HL_OF = {key: n for n, key in enumerate(HL)}
GATES = [(k, i) for k, i, _, _ in TILES if k == "gate"]
NORMS = [(k, i) for k, i, _, _ in TILES if k == "norm"]
VALS = [(k, i) for k, i, _, _ in TILES if k == "val"]

K_CAUSAL, K_TAIL, K_STRICT, K_CMP = 0, 128, 256, 384
K_MASKS = K_CMP + NT * CW
K_ID, K_BLOCK = K_MASKS, K_MASKS + P
K_ALL = K_BLOCK + P


def plan_units():
    units, pvs = [], []
    for h in range(HEADS):
        for pair in range(NT // 2):
            for branch in (("slc", "win", "cmp") if h < NSA_HEADS else ("sb",)):
                first = len(units)
                for q in (2 * pair, 2 * pair + 1):
                    k0 = max(0, q - WIN_TILES) if branch == "win" else 0
                    n = 1 if branch == "cmp" else q - k0 + 1
                    units.append((h, q, branch, k0, n, len(pvs)))
                pvs.append((h, pair, branch, first + 1))
    return units, pvs


UNITS, PVS = plan_units()
GROUPS, GROUP_END = [], []
for _u, (_h, _q, _b, _k0, _n, _v) in enumerate(UNITS):
    for _j in range(0, _n, 4):
        GROUPS.append((_u, _j, min(4, _n - _j)))
    GROUP_END.append(len(GROUPS))
GROUP_START = [0] + GROUP_END[:-1]
KSEQ = [("slc", 0), ("win", 0), ("slc", 1), ("win", 1)] + [("sb", h) for h in range(SB_HEADS)]
K_SLOTS = 3


def key_index(h, branch):
    return KSEQ.index((branch, h // GROUP)) if h < NSA_HEADS else KSEQ.index(("sb", h - NSA_HEADS))


K_LAST = [max(u for u, x in enumerate(UNITS) if x[2] != "cmp" and key_index(x[0], x[2]) == k) for k in range(len(KSEQ))]
HEAD_LAST = [max(u for u, x in enumerate(UNITS) if x[0] == h) for h in range(HEADS)]
OUTS = [v for v, x in enumerate(PVS) if x[2] in ("cmp", "sb")]
OUT_OF = {v: o for o, v in enumerate(OUTS)}
LAG_T = 3
LAG_PV = LAG_T + 2
LAG_OUT = LAG_PV + 1
PROB_SLOTS = LAG_T + 1
T_BANKS, O_BANKS = 2, 2
S_BANKS = 8 - T_BANKS - O_BANKS
STAT = 8
PV_AT = {x[3]: v for v, x in enumerate(PVS)}


def place_scores():
    at, users, out = 0, [-1] * S_BANKS, []
    for u, (_, _, branch, _, n, _) in enumerate(UNITS):
        need = 1 if branch == "cmp" else -(-n * P // HALF)
        if at + need > S_BANKS:
            at = 0
        out.append((at, max(users[at:at + need])))
        users[at:at + need] = [u] * need
        at = (at + need) % S_BANKS
    return out


SCORES = place_scores()
N_NSA = sum(x[2] != "sb" for x in UNITS)


def shape_constants():
    f = np.float32
    c = np.zeros((P, K_ALL), f)
    p, n = np.arange(P)[:, None], np.arange(P)[None, :]
    c[:, K_ID:K_ID + P] = p == n
    c[:, K_CAUSAL:K_CAUSAL + P] = np.where(n <= p, f(0), f(MASK))
    c[:, K_TAIL:K_TAIL + P] = np.where(n > p, f(0), f(MASK))
    c[:, K_STRICT:K_STRICT + P] = np.where(n < p, f(0), f(MASK))
    c[:, K_BLOCK:K_BLOCK + P] = (p // DH) == (n // DH)
    for q in range(NT):
        m = np.arange(CW)[None, :]
        ok = (m < N_CMP) & (m * CMP_STRIDE + CMP_LEN - 1 <= q * P + p)
        c[:, K_CMP + q * CW:K_CMP + (q + 1) * CW] = np.where(ok, f(0), f(MASK))
    half = ROPE // 2
    inv = np.power(f(500000.0), -np.arange(0, ROPE, 2, dtype=f) / f(ROPE)).astype(f)
    ang = (np.arange(S, dtype=f)[:, None] * inv[None, :]).astype(f)
    cos, sin = np.cos(ang).T.astype(f), np.sin(ang).T.astype(f)
    rot = np.zeros((2, P, S), f)
    rot[0] = 1
    for b in range(0, P, DH):
        rot[0, b:b + half], rot[0, b + half:b + ROPE] = cos, cos
        rot[1, b:b + half], rot[1, b + half:b + ROPE] = -sin, sin
    return c, rot


def build(nc, xT, norm_gain, w_in, q_norm_gain, k_norm_cmp, k_norm_slc, k_norm_win,
          cmp_k_pos, cmp_k_w1, cmp_k_b1, cmp_k_w2, cmp_v_pos, cmp_v_w1, cmp_v_b1, cmp_v_w2,
          w_out, consts, rotary, outT):
    ctx = ExitStack()
    with ctx:
        early = ExitStack()

        def sb(name, shape, dt=F32, where=ctx):
            return where.enter_context(nc.sbuf_tensor(name, shape, dt))

        def sem(name):
            return ctx.enter_context(nc.semaphore(name))

        hl_dram = nc.dram_tensor("hl_scratch", [len(HL), 2, P, S], F32, kind="Internal").ap()
        gate_dram = nc.dram_tensor("gate_scratch", [len(GATES), P, S], F32, kind="Internal").ap()
        val_dram = nc.dram_tensor("val_scratch", [4, P, NT, 2, P], F32, kind="Internal").ap()

        act_hi = sb("act_hi", [P, KT, S], F32R)
        act_lo = sb("act_lo", [P, KT, S], F32R)
        w_raw = sb("w_raw", [P, 2, KT, P])
        w_hi = sb("w_hi", [P, 2, KT, P], F32R)
        w_lo = sb("w_lo", [P, 2, KT, P], F32R)
        v_nsa = sb("v_nsa", [P, 2, NT, 2, P], F32R)
        v_cmp = sb("v_cmp", [CW, 2, P], F32R)
        kc_hh = sb("kc_hh", [P, 2, CW], F32R)
        kc_ll = sb("kc_ll", [P, 2, CW], F32R)
        ident = sb("ident", [P, P])
        masks = sb("masks", [P, K_MASKS + P], BF16)
        gate_tok = sb("gate_tok", [P, NT, NSA_HEADS * N_BRANCH])
        gain_x = sb("gain_x", [P, KT])
        gains = sb("gains", [P, 4])
        bias1 = sb("bias1", [P, 2])
        neg_max = sb("neg_max", [P, STAT])
        row_max = sb("row_max", [P, STAT])
        row_sum = sb("row_sum", [P, STAT])
        row_inv = sb("row_inv", [P, STAT])

        x_raw = sb("x_raw", [P, 2, S], where=early)
        raw2 = sb("raw2", [P, 2, S], where=early)
        normed = sb("normed", [P, S], where=early)
        square2 = sb("square2", [P, 2, S], where=early)
        inv_rms = sb("inv_rms", [P, S], where=early)
        swapped = sb("swapped", [P, S], where=early)
        token_inv = sb("token_inv", [P, S], where=early)
        part_hi = sb("part_hi", [P, 2, S], F32R, where=early)
        part_lo = sb("part_lo", [P, 2, S], F32R, where=early)
        gate_buf = sb("gate_buf", [P, S], where=early)
        v_buf = sb("v_buf", [P, NT, 2, P], F32R, where=early)
        rot = sb("rot", [P, 2, S], where=early)
        blocks_one = sb("blocks_one", [P, P], where=early)
        ones = sb("ones", [P, P], where=early)
        const_f = token_inv[:, 0:K_MASKS]
        w1 = sb("w1", [P, CMP_LEN, P], where=early)
        w2 = sb("w2", [P, 2, P], where=early)
        pos = sb("pos", [P, 2, CMP_LEN], where=early)
        x_slots = [x_raw[:, 0, :], x_raw[:, 1, :], gate_buf[:, :], inv_rms[:, :]]
        blk = x_raw[:, :, :].rearrange("p a (b c) -> p (a b) c", c=CW)
        hid = sb("hid", [P, 2, CW], where=early)
        sig = sb("sig", [P, 2, CW], where=early)
        kc_buf = sb("kc_buf", [P, 5, CW], where=early)
        kc_h = sb("kc_h", [P, CW], F32R, where=early)
        kc_l = sb("kc_l", [P, CW], F32R, where=early)
        early.close()

        pt_hi = sb("pt_hi", [P, 2, NT, 2 * P], F32R)
        pt_lo = sb("pt_lo", [P, 2, NT, 2 * P], F32R)
        prob = sb("prob", [P, PROB_SLOTS, S])
        keep = sb("keep", [P, 2, S + 1])
        q_st = sb("q_st", [P, 2, S], F32R)
        k_hh = sb("k_hh", [P, K_SLOTS, S], F32R)
        k_ll = sb("k_ll", [P, K_SLOTS, S], F32R)
        v_sb = v_nsa[:, :, :, 0, :]
        gate_st = sb("gate_st", [P, S])
        o_lo = sb("o_lo", [P, 2 * P])
        o_val = sb("o_val", [P, 2 * P])

        psum = ctx.enter_context(nc.psum_tensor("psum", [P, 8 * HALF], F32))
        ps_s = [psum[:, 0:2 * HALF], psum[:, 2 * HALF:4 * HALF]]
        ps_t = psum[:, 4 * HALF:6 * HALF]
        ps_o = [psum[:, 6 * HALF:7 * HALF], psum[:, 7 * HALF:8 * HALF]]
        pt_at, po_at = S_BANKS * HALF, (S_BANKS + T_BANKS) * HALF

        def score_cols(i, c, e):
            at = SCORES[i][0] * HALF
            return psum[:, at + c:at + e]

        def turned(g, rows, cols):
            at = pt_at + (g % T_BANKS) * HALF
            return psum[0:rows, at:at + cols]

        def result(o, r0, r1, c0, c1):
            at = po_at + (o % O_BANKS) * HALF
            return psum[r0:r1, at + c0:at + c1]

        s_const, s_small, s_w1 = sem("s_const"), sem("s_small"), sem("s_w1")
        s_cast, s_ones, s_zero = sem("s_cast"), sem("s_ones"), sem("s_zero")
        s_x = [sem(f"s_x{n}") for n in range(4)]
        s_xhi, s_xsq, s_xlo, s_xacc = sem("s_xhi"), sem("s_xsq"), sem("s_xlo"), sem("s_xacc")
        s_xms, s_xstd, s_tinv = sem("s_xms"), sem("s_xstd"), sem("s_tinv")
        s_w = [sem("s_wa"), sem("s_wb")]
        s_whi, s_wlo = sem("s_whi"), sem("s_wlo")
        s_proj, s_evac = sem("s_proj"), sem("s_evac")
        s_sq, s_ms, s_std, s_normed, s_swap, s_rot = (sem(n) for n in ("s_sq", "s_ms", "s_std", "s_normed", "s_swap", "s_rot"))
        s_phi, s_plo = sem("s_phi"), sem("s_plo")
        s_hl = [sem("s_hl0"), sem("s_hl1")]
        s_gsig, s_gate, s_gst = sem("s_gsig"), sem("s_gate"), sem("s_gst")
        s_vt, s_vhi, s_vlo, s_vst = (sem(n) for n in ("s_vt", "s_vhi", "s_vlo", "s_vst"))
        s_lsig, s_lt, s_ltok = sem("s_lsig"), sem("s_lt"), sem("s_ltok")
        s_blk, s_mlp, s_msig, s_hid, s_kv2 = (sem(n) for n in ("s_blk", "s_mlp", "s_msig", "s_hid", "s_kv2"))
        s_ksq, s_kms, s_kstd, s_kn, s_ksw, s_khi, s_klo, s_kst, s_vc = (
            sem(n) for n in ("s_ksq", "s_kms", "s_kstd", "s_kn", "s_ksw", "s_khi", "s_klo", "s_kst", "s_vc"))
        s_dve, s_act = sem("s_dve"), sem("s_act")
        s_ql = [sem("s_ql0"), sem("s_ql1")]
        s_kl = [sem(f"s_kl{i}") for i in range(K_SLOTS)]
        s_vl = [sem("s_vl0"), sem("s_vl1")]
        s_gl = sem("s_gl")
        s_score, s_nmax, s_exp, s_rinv, s_keep, s_p = (sem(n) for n in ("s_score", "s_nmax", "s_exp", "s_rinv", "s_keep", "s_p"))
        s_tr, s_hi, s_lo, s_pv, s_out = (sem(n) for n in ("s_tr", "s_hi", "s_lo", "s_pv", "s_out"))
        s_olo, s_oval, s_mhi, s_mix = sem("s_olo"), sem("s_oval"), sem("s_mhi"), sem("s_mix")
        s_xr = [sem("s_xr0"), sem("s_xr1")]
        s_y, s_st = sem("s_y"), [sem("s_st0"), sem("s_st1")]
        s_s1 = sem("s_s1")

        def chain(s):
            n = [0]

            def link(eng, ins):
                n[0] += 1
                ins.then_inc(s, 1)
                eng.wait_ge(s, n[0])
            return link

        w_in_v = w_in.rearrange("(k p) n -> p k n", p=P)
        w_out_v = w_out.rearrange("(k p) n -> p k n", p=P)
        xT_v = xT.rearrange("(k p) t -> k p t", p=P)
        outT_v = outT.rearrange("(k p) t -> k p t", p=P)

        def w_tile(t):
            if t < N_IN:
                _, _, c, m = TILES[t]
                return w_in_v[:, :, c:c + m], m
            return w_out_v[:, :, (t - N_IN) * P:(t - N_IN + 1) * P], P

        def values(b):
            return v_nsa[:, b] if b < 2 else v_buf[:, :, :, :]

        block = ctx.enter_context(nc.Block())

        @block.sync
        def _(sp):
            def load_w(t):
                if t >= 2:
                    sp.wait_ge(s_whi, t - 1)
                    sp.wait_ge(s_wlo, t - 1)
                src, m = w_tile(t)
                sp.dma_start(w_raw[:, t % 2, :, 0:m], src).then_inc(s_w[t % 2], 16)

            sp.dma_start(gain_x[:, :], norm_gain.rearrange("(k p) -> p k", p=P)).then_inc(s_small, 16)
            load_w(0)
            for k in range(KT):
                if k >= 4:
                    sp.wait_ge(s_xlo, k - 3)
                    sp.wait_ge(s_xsq, k - 3)
                sp.dma_start(x_slots[k % 4], xT_v[k]).then_inc(s_x[k % 4], 16)
            load_w(1)
            sp.dma_start(const_f, consts[:, 0:K_MASKS]).then_inc(s_const, 16)
            sp.dma_start(rot[:, :, :], rotary.rearrange("c p t -> p c t")).then_inc(s_const, 16)
            sp.dma_start(ident[:, :], consts[:, K_ID:K_ID + P]).then_inc(s_const, 16)
            sp.dma_start(blocks_one[:, :], consts[:, K_BLOCK:K_BLOCK + P]).then_inc(s_const, 16)
            for n, g in enumerate((q_norm_gain, k_norm_slc, k_norm_win, k_norm_cmp)):
                for b in range(0, P, DH):
                    sp.dma_start(gains[b:b + DH, n:n + 1], g.rearrange("(p a) -> p a", a=1)).then_inc(s_small, 16)
            for n, (b1, w2x, px) in enumerate(((cmp_k_b1, cmp_k_w2, cmp_k_pos), (cmp_v_b1, cmp_v_w2, cmp_v_pos))):
                for b in range(0, P, DH):
                    sp.dma_start(bias1[b:b + DH, n:n + 1], b1.rearrange("(p a) -> p a", a=1)).then_inc(s_small, 16)
                    if n == 0 and b == 0:
                        sp.wait_ge(s_zero, 2)
                    sp.dma_start(w2[b:b + DH, n, b:b + DH], w2x).then_inc(s_small, 16)
                    sp.dma_start(pos[b:b + DH, n, :], px.rearrange("l d -> d l")).then_inc(s_small, 16)

            def load_w1(n):
                src = (cmp_k_w1, cmp_v_w1)[n].rearrange("(l d) j -> d l j", d=DH)
                for b in range(0, P, DH):
                    sp.dma_start(w1[b:b + DH, :, b:b + DH], src).then_inc(s_w1, 16)
            load_w1(0)
            load_w(2)

            for t, (kind, i, _, _) in enumerate(TILES):
                if t + 3 < N_IN + 2:
                    load_w(t + 3)
                if kind == "cmp" and i == 1:
                    sp.wait_ge(s_mlp, 1)
                    load_w1(1)
                if kind == "norm":
                    n = NORMS.index((kind, i))
                    sp.wait_ge(s_normed, n + 1)
                    for b in range(0, P, DH):
                        sp.dma_start(swapped[b:b + 8, :], normed[b + 8:b + 16, :]).then_inc(s_swap, 16)
                        sp.dma_start(swapped[b + 8:b + 16, :], normed[b:b + 8, :]).then_inc(s_swap, 16)
                if (kind, i) in HL_OF:
                    u = HL_OF[kind, i]
                    sp.wait_ge(s_phi, u + 1)
                    sp.dma_start(hl_dram[u, 0], part_hi[:, u % 2, :].bitcast(F32)).then_inc(s_hl[u % 2], 16)
                    sp.wait_ge(s_plo, u + 1)
                    sp.dma_start(hl_dram[u, 1], part_lo[:, u % 2, :].bitcast(F32)).then_inc(s_hl[u % 2], 16)
                if kind == "gate":
                    sp.wait_ge(s_gate, GATES.index((kind, i)) + 1)
                    sp.dma_start(gate_dram[i], gate_buf[:, :]).then_inc(s_gst, 16)
                if kind == "val" and i >= 2:
                    sp.wait_ge(s_vhi, i + 1)
                    sp.wait_ge(s_vlo, i + 1)
                    sp.dma_start(val_dram[i - 2], v_buf[:, :, :, :].bitcast(F32)).then_inc(s_vst, 16)
                if kind == "cmp" and i == 0:
                    sp.wait_ge(s_kn, 1)
                    for b in range(0, P, DH):
                        sp.dma_start(kc_buf[b:b + 8, 3, 0:N_CMP], kc_buf[b + 8:b + 16, 2, 0:N_CMP]).then_inc(s_ksw, 16)
                        sp.dma_start(kc_buf[b + 8:b + 16, 3, 0:N_CMP], kc_buf[b:b + 8, 2, 0:N_CMP]).then_inc(s_ksw, 16)
                    sp.wait_ge(s_khi, 1)
                    sp.wait_ge(s_klo, 1)
                    for g in range(KV_HEADS):
                        for b in range(0, P, DH):
                            sp.dma_start(kc_hh[b:b + DH, g, :].bitcast(F32), kc_h[g * DH:(g + 1) * DH, :].bitcast(F32)).then_inc(s_kst, 16)
                            sp.dma_start(kc_ll[b:b + DH, g, :].bitcast(F32), kc_l[g * DH:(g + 1) * DH, :].bitcast(F32)).then_inc(s_kst, 16)

            sp.wait_ge(s_s1, 4)
            for n in range(2):
                sp.wait_ge(s_hl[n], 32 * len(range(n, len(HL), 2)))
            sp.wait_ge(s_gst, 16 * len(GATES))
            sp.wait_ge(s_vst, 16 * 4)
            nc.sync.sem_inc(s_s1, 1)

            def stacks(dst, slot, s, tile, row, order):
                for b, part in zip((0, DH), order):
                    sp.dma_start(dst[b:b + DH, slot, :].bitcast(F32), hl_dram[tile, part, row:row + DH, :]).then_inc(s, 16)

            def load_keys(k):
                branch, i = KSEQ[k]
                if k >= K_SLOTS:
                    sp.wait_ge(s_score, K_LAST[k - K_SLOTS] + 1)
                tile = HL_OF["sbk", i // 2] if branch == "sb" else HL_OF["norm", 0 if branch == "slc" else 1]
                stacks(k_hh, k % K_SLOTS, s_kl[k % K_SLOTS], tile, (i % 2) * DH, (0, 0))
                stacks(k_ll, k % K_SLOTS, s_kl[k % K_SLOTS], tile, (i % 2) * DH, (1, 1))

            def load_queries(h):
                if h >= 2:
                    sp.wait_ge(s_score, HEAD_LAST[h - 2] + 1)
                tile = HL_OF["norm", 2 + h // 2] if h < NSA_HEADS else HL_OF["sbq", (h - NSA_HEADS) // 2]
                stacks(q_st, h % 2, s_ql[h % 2], tile, (h % 2) * DH, (0, 1))

            def load_values(h):
                n = h - NSA_HEADS
                if n >= 2:
                    sp.wait_ge(s_pv, max(v for v, x in enumerate(PVS) if x[0] == h - 2) + 1)
                sp.dma_start(v_sb[:, n % 2].bitcast(F32), val_dram[n // 2, :, :, n % 2, :]).then_inc(s_vl[n % 2], 16)

            def load_gate(t):
                if t >= 1:
                    sp.wait_ge(s_mix, (NT // 2) * 2 * t)
                sp.dma_start(gate_st[:, :], gate_dram[t]).then_inc(s_gl, 16)

            load_queries(0)
            load_keys(0)
            load_keys(1)
            load_gate(0)
            load_keys(2)
            for h in range(HEADS):
                if h + 1 < HEADS:
                    load_queries(h + 1)
                if h == 3:
                    load_keys(3)
                if h >= NSA_HEADS - 1 and h + 1 < HEADS:
                    if h + 1 == NSA_HEADS:
                        load_keys(4)
                    load_values(h + 1)
                    if h + 2 < HEADS:
                        load_keys(h + 2 - NSA_HEADS + 4)
                if h % 2 == 1 and h + 1 < HEADS:
                    load_gate((h + 1) // 2)

            sp.wait_ge(s_mix, HEADS * (NT // 2))
            for t in range(N_OUT):
                if t + 2 < N_OUT:
                    load_w(N_IN + t + 2)
                if t >= 2:
                    sp.wait_ge(s_st[t % 2], 16 * (t // 2))
                sp.dma_start(prob[:, t % 2, :], xT_v[t]).then_inc(s_xr[t % 2], 16)
                sp.wait_ge(s_y, t + 1)
                sp.dma_start(outT_v[t], prob[:, t % 2, :]).then_inc(s_st[t % 2], 16)
            for n in range(2):
                sp.wait_ge(s_st[n], 16 * (N_OUT // 2))

        @block.gpsimd
        def _(pool):
            nc.gpsimd.memset(ones[:, :], 1.0).then_inc(s_ones, 1)
            nc.gpsimd.memset(w2[:, :, :], 0.0).then_inc(s_zero, 1)
            nc.gpsimd.memset(w1[:, :, :], 0.0).then_inc(s_zero, 1)
            nc.gpsimd.memset(swapped[:, :], 0.0).then_inc(s_zero, 1)
            nc.gpsimd.memset(kc_buf[:, :, :], 0.0).then_inc(s_zero, 1)

            def split_lo(t):
                pool.wait_ge(s_w[t % 2], 16 * (t // 2 + 1))
                pool.wait_ge(s_whi, t + 1)
                if t >= 2:
                    pool.wait_ge(s_proj, t - 1)
                m = w_tile(t)[1]
                nc.gpsimd.tensor_tensor(w_lo[:, t % 2, :, 0:m], w_raw[:, t % 2, :, 0:m],
                                        w_hi[:, t % 2, :, 0:m].bitcast(F32), ALU.subtract).then_inc(s_wlo, 1)

            for t in range(N_IN):
                split_lo(t)
            pool.wait_ge(s_mlp, 2)
            pool.wait_ge(s_ltok, 1)
            nc.gpsimd.sem_inc(s_s1, 1)
            for t in range(N_IN, N_IN + 2):
                split_lo(t)
            pool.wait_ge(s_s1, 5)
            for n in range(2):
                nc.gpsimd.memset(keep[:, n, S:S + 1], 1.0).then_inc(s_ones, 1)
            for i, (h, q, branch, k0, n, v) in enumerate(UNITS):
                w = CW if branch == "cmp" else n * P
                a = prob[:, i % PROB_SLOTS, 0:w]
                if branch == "sb":
                    m = i - N_NSA
                    pool.wait_ge(s_keep, m + 1)
                    nc.gpsimd.tensor_tensor(a, a, keep[:, m % 2, S - w + 1:S + 1], ALU.mult).then_inc(s_p, 1)
                else:
                    b = ("cmp", "slc", "win").index(branch)
                    pool.wait_ge(s_rinv, i + 1)
                    nc.gpsimd.tensor_scalar(a, a, row_inv[:, i % STAT:i % STAT + 1],
                                            gate_tok[:, q, h * N_BRANCH + b:h * N_BRANCH + b + 1],
                                            ALU.mult, ALU.mult).then_inc(s_p, 1)
            for t in range(N_IN + 2, N_IN + N_OUT):
                split_lo(t)

        @block.scalar
        def _(act):
            link = chain(s_act)
            func = nc.scalar.activation

            def split_hi(t):
                act.wait_ge(s_w[t % 2], 16 * (t // 2 + 1))
                if t >= 2:
                    act.wait_ge(s_proj, t - 1)
                    act.wait_ge(s_wlo, t - 1)
                m = w_tile(t)[1]
                func(w_hi[:, t % 2, :, 0:m], w_raw[:, t % 2, :, 0:m], ACT.Copy).then_inc(s_whi, 1)

            act.wait_ge(s_small, 16)
            split_hi(0)
            for k in range(KT):
                act.wait_ge(s_x[k % 4], 16 * (k // 4 + 1))
                func(act_hi[:, k, :], x_slots[k % 4], ACT.Copy, scale=gain_x[:, k:k + 1]).then_inc(s_xhi, 1)
                if k >= 2:
                    act.wait_ge(s_xacc, k - 1)
                func(square2[:, k % 2, :], x_slots[k % 4], ACT.Square).then_inc(s_xsq, 1)
            split_hi(1)
            act.wait_ge(s_const, 64)
            func(masks[:, 0:K_MASKS], const_f, ACT.Copy).then_inc(s_cast, 1)
            func(masks[:, K_MASKS:K_MASKS + P], ident[:, :], ACT.Copy).then_inc(s_cast, 1)
            act.wait_ge(s_xms, 1)
            act.wait_ge(s_cast, 2)
            func(token_inv[:, :], ps_t[:, :], ACT.Sqrt, scale=1.0 / D, bias=EPS).then_inc(s_xstd, 1)

            def first(t):
                kind, i, _, m = TILES[t]
                act.wait_ge(s_evac, t + 1)
                raw, square = raw2[:, t % 2, :], square2[:, t % 2, :]
                if kind == "norm":
                    func(square, raw, ACT.Square).then_inc(s_sq, 1)
                elif kind == "gate":
                    func(square, raw, ACT.Sigmoid).then_inc(s_gsig, 1)
                elif kind == "logit":
                    func(square[0:m, :], raw[0:m, :], ACT.Sigmoid).then_inc(s_lsig, 1)

            def root(t):
                kind, i, _, _ = TILES[t]
                if kind == "norm":
                    act.wait_ge(s_ms, NORMS.index((kind, i)) + 1)
                    func(inv_rms[:, :], ps_t, ACT.Sqrt, scale=1.0 / DH, bias=EPS).then_inc(s_std, 1)

            def last(t):
                kind, i, _, _ = TILES[t]
                if (kind, i) in HL_OF:
                    u = HL_OF[kind, i]
                    if kind == "norm":
                        act.wait_ge(s_rot, NORMS.index((kind, i)) + 1)
                    if u >= 2:
                        act.wait_ge(s_hl[u % 2], 32 * (u // 2))
                    func(part_hi[:, u % 2, :], raw2[:, t % 2, :], ACT.Copy).then_inc(s_phi, 1)
                elif kind == "val":
                    act.wait_ge(s_vt, i + 1)
                    if i >= 3:
                        act.wait_ge(s_vst, 16 * (i - 2))
                    dst = values(i).rearrange("p a b c -> p (a b) c")
                    func(dst[:, :, 0:DH], ps_t.rearrange("p (a c) -> p a c", c=DH), ACT.Copy).then_inc(s_vhi, 1)
                elif kind == "cmp":
                    act.wait_ge(s_mlp, i + 1)
                    func(sig[:, i, 0:N_CMP], ps_o[i][:, 0:N_CMP], ACT.Sigmoid, bias=bias1[:, i:i + 1]).then_inc(s_msig, 1)
                    act.wait_ge(s_kv2, i + 1)
                    if i == 0:
                        link(act, func(kc_buf[:, 0, 0:N_CMP], ps_o[0][:, 64:64 + N_CMP], ACT.Copy))
                        func(kc_buf[:, 1, 0:N_CMP], kc_buf[:, 0, 0:N_CMP], ACT.Square).then_inc(s_ksq, 1)
                        act.wait_ge(s_kms, 1)
                        func(kc_buf[:, 1, 0:N_CMP], ps_o[0][:, 128:128 + N_CMP], ACT.Sqrt, scale=1.0 / DH, bias=EPS).then_inc(s_kstd, 1)
                        act.wait_ge(s_kn, 2)
                        func(kc_h[:, :], kc_buf[:, 4, :], ACT.Copy).then_inc(s_khi, 1)
                    else:
                        func(v_cmp[0:N_CMP, :, 0:DH], ps_o[1][0:N_CMP, 128:256].rearrange("p (g c) -> p g c", c=DH),
                             ACT.Copy).then_inc(s_vc, 1)

            for t in range(N_IN):
                first(t)
                split_hi(t + 2)
                if t >= 1:
                    last(t - 1)
                root(t)
            last(N_IN - 1)
            nc.scalar.sem_inc(s_s1, 1)

            act.wait_ge(s_s1, 5)
            act.wait_ge(s_ones, 3)

            def weights(i):
                h, q, branch, k0, n, v = UNITS[i]
                w = CW if branch == "cmp" else n * P
                if i >= PROB_SLOTS:
                    act.wait_ge(s_tr, GROUP_END[i - PROB_SLOTS])
                if branch == "sb":
                    m = i - N_NSA
                    act.wait_ge(s_score, i + 1)
                    if m >= 2:
                        act.wait_ge(s_p, i - 1)
                    func(keep[:, m % 2, S - w:S], score_cols(i, 0, w), ACT.Sigmoid, scale=-1.0)
                    func(prob[:, i % PROB_SLOTS, 0:w], score_cols(i, 0, w), ACT.Sigmoid).then_inc(s_exp, 1)
                else:
                    act.wait_ge(s_nmax, i + 1)
                    func(prob[:, i % PROB_SLOTS, 0:w], score_cols(i, 0, w), ACT.Exp, bias=neg_max[:, i % STAT:i % STAT + 1],
                         accum_out=row_sum[:, i % STAT:i % STAT + 1]).then_inc(s_exp, 1)

            def transposed_hi(i):
                h, q, branch, k0, n, v = UNITS[i]
                for g in range(GROUP_START[i], GROUP_END[i]):
                    _, j, c = GROUPS[g]
                    rows = CW if branch == "cmp" else P
                    act.wait_ge(s_tr, g + 1)
                    if v >= 2:
                        act.wait_ge(s_pv, v - 1)
                    func(pt_hi[0:rows, v % 2, k0 + j:k0 + j + c, (q % 2) * P:(q % 2 + 1) * P],
                         turned(g, rows, c * P).rearrange("p (a b) -> p a b", b=P), ACT.Copy).then_inc(s_hi, 1)

            def output_hi(v):
                h, pair, _, _ = PVS[v]
                o, b = OUT_OF[v], (h % 2) * DH
                act.wait_ge(s_out, o + 1)
                if o >= 1:
                    act.wait_ge(s_oval, 2 * o)
                func(o_lo[b:b + DH, :], result(o, DH, P, 0, 2 * P), ACT.Copy).then_inc(s_olo, 1)
                act.wait_ge(s_oval, 2 * (o + 1))
                func(act_hi[b:b + DH, h // 2, pair * 2 * P:(pair + 1) * 2 * P], o_val[b:b + DH, :], ACT.Copy).then_inc(s_mhi, 1)

            for i in range(len(UNITS) + LAG_OUT):
                if 0 <= i - LAG_T < len(UNITS):
                    transposed_hi(i - LAG_T)
                if i < len(UNITS):
                    weights(i)
                if i - LAG_OUT in PV_AT and PV_AT[i - LAG_OUT] in OUT_OF:
                    output_hi(PV_AT[i - LAG_OUT])
            for t in range(N_IN + 2, N_IN + N_OUT):
                split_hi(t)

        @block.vector
        def _(dve):
            link = chain(s_dve)
            tt, ts, stt = nc.vector.tensor_tensor, nc.vector.tensor_scalar, nc.vector.scalar_tensor_tensor
            dve.wait_ge(s_small, 16)
            for k in range(KT):
                dve.wait_ge(s_xhi, k + 1)
                stt(act_lo[:, k, :], x_slots[k % 4], gain_x[:, k:k + 1], act_hi[:, k, :].bitcast(F32),
                    ALU.mult, ALU.subtract).then_inc(s_xlo, 1)
                dve.wait_ge(s_xsq, k + 1)
                if k == 0:
                    nc.vector.tensor_copy(normed[:, :], square2[:, 0, :]).then_inc(s_xacc, 1)
                else:
                    dve.wait_ge(s_xacc, k)
                    tt(normed[:, :], normed[:, :], square2[:, k % 2, :], ALU.add).then_inc(s_xacc, 1)
            dve.wait_ge(s_small, 16 * (1 + 8 + 12))
            link(dve, ts(gains[:, 0:1], gains[:, 0:1], SCALE, None, ALU.mult))
            dve.wait_ge(s_xstd, 1)
            nc.vector.reciprocal(token_inv[:, :], token_inv[:, :]).then_inc(s_tinv, 1)
            dve.wait_ge(s_tinv, 1)

            def evacuate(t):
                kind, _, _, m = TILES[t]
                dve.wait_ge(s_proj, t + 1)
                raw = raw2[:, t % 2, :]
                for half in range(2):
                    c = slice(half * HALF, (half + 1) * HALF)
                    if kind == "sbq":
                        ins = stt(raw[0:m, c], ps_s[t % 2][0:m, c], SCALE, token_inv[0:m, c], ALU.mult, ALU.mult)
                    else:
                        ins = tt(raw[0:m, c], ps_s[t % 2][0:m, c], token_inv[0:m, c], ALU.mult)
                ins.then_inc(s_evac, 1)
                dve.wait_ge(s_evac, t + 1)

            def normalise(t):
                kind, i, _, _ = TILES[t]
                if kind == "norm":
                    n = NORMS.index((kind, i))
                    gain = gains[:, i + 1:i + 2] if i < 2 else gains[:, 0:1]
                    dve.wait_ge(s_std, n + 1)
                    link(dve, nc.vector.reciprocal(inv_rms[:, :], inv_rms[:, :]))
                    stt(normed[:, :], raw2[:, t % 2, :], gain, inv_rms[:, :], ALU.mult, ALU.mult).then_inc(s_normed, 1)
                    dve.wait_ge(s_normed, n + 1)
                elif kind == "cmp":
                    raw = raw2[:, t % 2, :]
                    if i == 0:
                        dve.wait_ge(s_zero, 4)
                    else:
                        dve.wait_ge(s_mlp, 1)
                    tokens = raw.rearrange("p (n l) -> p l n", l=CMP_STRIDE)
                    for a in range(CMP_LEN // CMP_STRIDE):
                        ls = slice(a * CMP_STRIDE, (a + 1) * CMP_STRIDE)
                        where = pos[:, i, ls].rearrange("p (l o) -> p l o", o=1).broadcast_to([P, CMP_STRIDE, N_CMP])
                        ins = tt(blk[:, ls, 0:N_CMP], tokens[:, :, a:a + N_CMP], where, ALU.add)
                    ins.then_inc(s_blk, 1)

            def finish(t):
                kind, i, _, m = TILES[t]
                raw, square = raw2[:, t % 2, :], square2[:, t % 2, :]
                if kind == "norm":
                    n = NORMS.index((kind, i))
                    link(dve, tt(raw, normed[:, :], rot[:, 0, :], ALU.mult))
                    dve.wait_ge(s_swap, 64 * (n + 1))
                    link(dve, tt(swapped[:, :], swapped[:, :], rot[:, 1, :], ALU.mult))
                    tt(raw, raw, swapped[:, :], ALU.add).then_inc(s_rot, 1)
                    dve.wait_ge(s_rot, n + 1)
                if (kind, i) in HL_OF:
                    u = HL_OF[kind, i]
                    dve.wait_ge(s_phi, u + 1)
                    tt(part_lo[:, u % 2, :], raw, part_hi[:, u % 2, :].bitcast(F32), ALU.subtract).then_inc(s_plo, 1)
                    dve.wait_ge(s_plo, u + 1)
                elif kind == "gate":
                    n = GATES.index((kind, i))
                    dve.wait_ge(s_gsig, n + 1)
                    if n >= 1:
                        dve.wait_ge(s_gst, 16 * n)
                    tt(gate_buf[:, :], raw, square, ALU.mult).then_inc(s_gate, 1)
                    dve.wait_ge(s_gate, n + 1)
                elif kind == "logit":
                    dve.wait_ge(s_lt, 1)
                    nc.vector.tensor_copy(gate_tok[:, :, :], ps_t[:, 0:NT * m].rearrange("p (a b) -> p a b", b=m)).then_inc(s_ltok, 1)
                elif kind == "val":
                    dve.wait_ge(s_vhi, i + 1)
                    dst = values(i).rearrange("p a b c -> p (a b) c")
                    tt(dst[:, :, DH:P], ps_t.rearrange("p (a c) -> p a c", c=DH), dst[:, :, 0:DH].bitcast(F32),
                       ALU.subtract).then_inc(s_vlo, 1)
                    dve.wait_ge(s_vlo, i + 1)
                elif kind == "cmp":
                    dve.wait_ge(s_msig, i + 1)
                    stt(hid[:, i, 0:N_CMP], ps_o[i][:, 0:N_CMP], bias1[:, i:i + 1], sig[:, i, 0:N_CMP],
                        ALU.add, ALU.mult).then_inc(s_hid, 1)
                    if i == 0:
                        dve.wait_ge(s_kstd, 1)
                        link(dve, nc.vector.reciprocal(kc_buf[:, 1, 0:N_CMP], kc_buf[:, 1, 0:N_CMP]))
                        stt(kc_buf[:, 2, 0:N_CMP], kc_buf[:, 0, 0:N_CMP], gains[:, 3:4], kc_buf[:, 1, 0:N_CMP],
                            ALU.mult, ALU.mult).then_inc(s_kn, 1)
                        dve.wait_ge(s_kn, 1)
                        ends = rot[:, :, CMP_LEN - 1:S:CMP_STRIDE]
                        dve.wait_ge(s_ksw, 64)
                        link(dve, tt(kc_buf[:, 0, 0:N_CMP], kc_buf[:, 2, 0:N_CMP], ends[:, 0, :], ALU.mult))
                        link(dve, tt(kc_buf[:, 3, 0:N_CMP], kc_buf[:, 3, 0:N_CMP], ends[:, 1, :], ALU.mult))
                        tt(kc_buf[:, 4, 0:N_CMP], kc_buf[:, 0, 0:N_CMP], kc_buf[:, 3, 0:N_CMP], ALU.add).then_inc(s_kn, 1)
                        dve.wait_ge(s_kn, 2)
                        dve.wait_ge(s_khi, 1)
                        tt(kc_l[:, :], kc_buf[:, 4, :], kc_h[:, :].bitcast(F32), ALU.subtract).then_inc(s_klo, 1)
                        link(dve, nc.vector.memset(v_cmp[:, :, :].bitcast(mybir.dt.uint32), 0))
                    else:
                        dve.wait_ge(s_vc, 1)
                        tt(v_cmp[0:N_CMP, :, DH:P], ps_o[1][0:N_CMP, 128:256].rearrange("p (g c) -> p g c", c=DH),
                           v_cmp[0:N_CMP, :, 0:DH].bitcast(F32), ALU.subtract).then_inc(s_vc, 1)

            for t in range(N_IN):
                evacuate(t)
                if t >= 1:
                    finish(t - 1)
                normalise(t)
            finish(N_IN - 1)
            nc.vector.sem_inc(s_s1, 1)
            dve.wait_ge(s_s1, 5)

            def maximum(i):
                h, q, branch, k0, n, v = UNITS[i]
                w = CW if branch == "cmp" else n * P
                c = slice(i % STAT, i % STAT + 1)
                dve.wait_ge(s_score, i + 1)
                link(dve, nc.vector.tensor_reduce(row_max[:, c], score_cols(i, 0, w), AX_X, ALU.max))
                if i >= STAT:
                    dve.wait_ge(s_exp, i - STAT + 1)
                ts(neg_max[:, c], row_max[:, c], -1.0, NEG_MAX_CAP, ALU.mult, ALU.min).then_inc(s_nmax, 1)

            def row_factor(i):
                h, q, branch, k0, n, v = UNITS[i]
                c = slice(i % STAT, i % STAT + 1)
                dve.wait_ge(s_exp, i + 1)
                if branch == "sb":
                    w, m = n * P, i - N_NSA
                    row = keep[:, m % 2, S - w:S][:, ::-1]
                    nc.vector.tensor_tensor_scan(row, row, row, 1.0, ALU.mult, ALU.bypass).then_inc(s_keep, 1)
                    return
                if i >= STAT:
                    dve.wait_ge(s_p, i - STAT + 1)
                if branch == "cmp":
                    link(dve, ts(row_sum[:, c], row_sum[:, c], 1e-30, None, ALU.max))
                nc.vector.reciprocal(row_inv[:, c], row_sum[:, c]).then_inc(s_rinv, 1)

            def transposed_lo(i):
                h, q, branch, k0, n, v = UNITS[i]
                for g in range(GROUP_START[i], GROUP_END[i]):
                    _, j, c = GROUPS[g]
                    rows = CW if branch == "cmp" else P
                    at = (slice(0, rows), v % 2, slice(k0 + j, k0 + j + c), slice((q % 2) * P, (q % 2 + 1) * P))
                    dve.wait_ge(s_hi, g + 1)
                    tt(pt_lo[at], turned(g, rows, c * P).rearrange("p (a b) -> p a b", b=P),
                       pt_hi[at].bitcast(F32), ALU.subtract).then_inc(s_lo, 1)

            def output(v):
                h, pair, _, _ = PVS[v]
                o, b, cols = OUT_OF[v], (h % 2) * DH, slice(pair * 2 * P, (pair + 1) * 2 * P)
                dve.wait_ge(s_olo, o + 1)
                if o >= 1:
                    dve.wait_ge(s_mhi, o)
                    dve.wait_ge(s_mix, o)
                tt(o_val[b:b + DH, :], result(o, 0, DH, 0, 2 * P), o_lo[b:b + DH, :], ALU.add).then_inc(s_oval, 1)
                dve.wait_ge(s_oval, 2 * o + 1)
                dve.wait_ge(s_gl, 16 * (h // 2 + 1))
                tt(o_val[b:b + DH, :], o_val[b:b + DH, :], gate_st[b:b + DH, cols], ALU.mult).then_inc(s_oval, 1)
                dve.wait_ge(s_mhi, o + 1)
                tt(act_lo[b:b + DH, h // 2, cols], o_val[b:b + DH, :], act_hi[b:b + DH, h // 2, cols].bitcast(F32),
                   ALU.subtract).then_inc(s_mix, 1)

            for i in range(len(UNITS) + LAG_OUT):
                if i < N_NSA:
                    maximum(i)
                if 1 <= i <= len(UNITS):
                    row_factor(i - 1)
                if 0 <= i - LAG_T < len(UNITS):
                    transposed_lo(i - LAG_T)
                if i - LAG_OUT in PV_AT and PV_AT[i - LAG_OUT] in OUT_OF:
                    output(PV_AT[i - LAG_OUT])
            for t in range(N_OUT):
                dve.wait_ge(s_xr[t % 2], 16 * (t // 2 + 1))
                dve.wait_ge(s_proj, N_IN + t + 1)
                for half in range(2):
                    c = slice(half * HALF, (half + 1) * HALF)
                    ins = tt(prob[:, t % 2, c], ps_s[t % 2][:, c], prob[:, t % 2, c], ALU.add)
                ins.then_inc(s_y, 1)

        @block.tensor
        def _(pe):
            mm = nc.tensor.matmul

            def project(t, half, slot):
                m = w_tile(t)[1]
                c = slice(half * HALF, (half + 1) * HALF)
                for k in range(KT):
                    if t == 0:
                        pe.wait_ge(s_xhi, k + 1)
                        pe.wait_ge(s_xlo, k + 1)
                    for n, (w, a) in enumerate(((w_hi, act_hi), (w_hi, act_lo), (w_lo, act_hi))):
                        ins = mm(ps_s[slot][0:m, c], w[:, t % 2, k, 0:m], a[:, k, c],
                                 start=(k == 0 and n == 0), stop=(k == KT - 1 and n == 2))
                return ins

            def side_work(t):
                kind, i, _, m = TILES[t]
                if kind in ("norm", "val", "logit"):
                    before = [x for x in TILES[:t] if x[0] in ("norm", "val", "logit")]
                    if not before:
                        pe.wait_ge(s_xstd, 1)
                    elif before[-1][0] == "norm":
                        pe.wait_ge(s_std, NORMS.index(before[-1][0:2]) + 1)
                    elif before[-1][0] == "val":
                        pe.wait_ge(s_vlo, before[-1][1] + 1)
                    else:
                        pe.wait_ge(s_ltok, 1)
                if kind == "norm":
                    pe.wait_ge(s_sq, NORMS.index((kind, i)) + 1)
                    for half in range(2):
                        c = slice(half * HALF, (half + 1) * HALF)
                        ins = mm(ps_t[:, c], blocks_one[:, :], square2[:, t % 2, c], start=True, stop=True)
                    ins.then_inc(s_ms, 1)
                elif kind == "val":
                    pe.wait_ge(s_evac, t + 1)
                    for j in range(NT):
                        ins = nc.tensor.transpose(ps_t[:, j * P:(j + 1) * P], raw2[:, t % 2, j * P:(j + 1) * P], ident[:, :])
                    ins.then_inc(s_vt, 1)
                elif kind == "logit":
                    pe.wait_ge(s_lsig, 1)
                    for j in range(NT):
                        ins = nc.tensor.transpose(ps_t[:, j * m:(j + 1) * m], square2[0:m, t % 2, j * P:(j + 1) * P], ident[0:m, 0:m])
                    ins.then_inc(s_lt, 1)
                elif kind == "cmp":
                    pe.wait_ge(s_w1, 32 * (i + 1))
                    pe.wait_ge(s_blk, i + 1)
                    for l in range(CMP_LEN):
                        ins = mm(ps_o[i][:, 0:N_CMP], w1[:, l, :], blk[:, l, 0:N_CMP], start=(l == 0), stop=(l == CMP_LEN - 1))
                    ins.then_inc(s_mlp, 1)

            def second_layer(t):
                kind, i, _, _ = TILES[t]
                if kind == "cmp":
                    pe.wait_ge(s_hid, i + 1)
                    if i == 0:
                        mm(ps_o[0][:, 64:64 + N_CMP], w2[:, 0, :], hid[:, 0, 0:N_CMP], start=True, stop=True).then_inc(s_kv2, 1)
                    else:
                        mm(ps_o[1][0:N_CMP, 128:256], hid[:, 1, 0:N_CMP], w2[:, 1, :], start=True, stop=True).then_inc(s_kv2, 1)

            def compressed_norm(t):
                if TILES[t][0:2] == ("cmp", 0):
                    pe.wait_ge(s_ksq, 1)
                    mm(ps_o[0][:, 128:128 + N_CMP], blocks_one[:, :], kc_buf[:, 1, 0:N_CMP], start=True, stop=True).then_inc(s_kms, 1)

            for t in range(N_IN):
                pe.wait_ge(s_whi, t + 1)
                pe.wait_ge(s_wlo, t + 1)
                if t >= 2:
                    pe.wait_ge(s_evac, t - 1)
                project(t, 0, t % 2)
                if t == 0:
                    pe.wait_ge(s_ones, 1)
                    pe.wait_ge(s_xacc, KT)
                    for half in range(2):
                        c = slice(half * HALF, (half + 1) * HALF)
                        ins = mm(ps_t[:, c], ones[:, :], normed[:, c], start=True, stop=True)
                    ins.then_inc(s_xms, 1)
                else:
                    if t >= 2:
                        second_layer(t - 2)
                    side_work(t - 1)
                project(t, 1, t % 2).then_inc(s_proj, 1)
                if t >= 2:
                    compressed_norm(t - 2)
            side_work(N_IN - 1)
            nc.tensor.sem_inc(s_s1, 1)
            pe.wait_ge(s_s1, 5)
            pe.wait_ge(s_kst, 128)
            pe.wait_ge(s_cast, 2)
            pe.wait_ge(s_vc, 2)
            id_b = masks[:, K_MASKS:K_MASKS + P]

            def scores(i):
                h, q, branch, k0, n, v = UNITS[i]
                if SCORES[i][1] >= 0:
                    pe.wait_ge(s_exp, SCORES[i][1] + 1)
                pe.wait_ge(s_ql[h % 2], 32 * (h // 2 + 1))
                if branch == "cmp":
                    hh, ll, w, masked = kc_hh[:, h // GROUP, :], kc_ll[:, h // GROUP, :], CW, {0: (K_CMP + q * CW, CW)}
                else:
                    k = key_index(h, branch)
                    pe.wait_ge(s_kl[k % K_SLOTS], 64 * (k // K_SLOTS + 1))
                    hh, ll, w = k_hh[:, k % K_SLOTS, k0 * P:(k0 + n) * P], k_ll[:, k % K_SLOTS, k0 * P:(k0 + n) * P], n * P
                    masked = {w - P: (K_STRICT if branch == "sb" else K_CAUSAL, P)}
                    if branch == "win" and q >= WIN_TILES:
                        masked[0] = (K_TAIL, P)
                qs = q_st[:, h % 2, q * P:(q + 1) * P]
                for c in range(0, w, HALF):
                    e = min(w, c + HALF)
                    mm(score_cols(i, c, e), qs, hh[:, c:e], start=True, stop=False)
                    for at, (col, mw) in masked.items():
                        if c <= at < e:
                            mm(score_cols(i, at, at + mw), id_b, masks[:, col:col + mw], start=False, stop=False)
                    ins = mm(score_cols(i, c, e), qs, ll[:, c:e], start=False, stop=True)
                ins.then_inc(s_score, 1)

            def transposes(i):
                h, q, branch, k0, n, v = UNITS[i]
                pe.wait_ge(s_p, i + 1)
                for g in range(GROUP_START[i], GROUP_END[i]):
                    _, j, c = GROUPS[g]
                    if g >= T_BANKS:
                        pe.wait_ge(s_lo, g - T_BANKS + 1)
                    for a in range(c):
                        to = turned(g, CW if branch == "cmp" else P, 4 * P)[:, a * P:(a + 1) * P]
                        if branch == "cmp":
                            ins = nc.tensor.transpose(to, prob[:, i % PROB_SLOTS, 0:CW], ident[:, :])
                        else:
                            ins = nc.tensor.transpose(to, prob[:, i % PROB_SLOTS, (j + a) * P:(j + a + 1) * P], ident[:, :])
                    ins.then_inc(s_tr, 1)

            def weighted_values(v):
                h, pair, branch, last = PVS[v]
                nth = len([x for x in OUTS if x < v])
                pe.wait_ge(s_lo, GROUP_END[last])
                first = branch in ("slc", "sb")
                if first and nth >= O_BANKS:
                    pe.wait_ge(s_oval, 2 * (nth - O_BANKS + 1))
                if branch == "cmp":
                    jobs = [(0, 0, 2 * P)]
                else:
                    k0 = [UNITS[last - 1][3], UNITS[last][3]]
                    jobs = []
                    for j in range(min(k0), 2 * pair + 2):
                        lo = 0 if j <= 2 * pair else P
                        hi = 2 * P if j >= k0[1] else P
                        jobs.append((j, lo, hi))
                if branch == "sb":
                    n = h - NSA_HEADS
                    pe.wait_ge(s_vl[n % 2], 16 * (n // 2 + 1))
                final = v in OUT_OF
                for n, (j, lo, hi) in enumerate(jobs):
                    if branch == "cmp":
                        rows, val = CW, v_cmp[:, h // GROUP, :]
                    elif branch == "sb":
                        rows, val = P, v_sb[:, (h - NSA_HEADS) % 2, j, :]
                    else:
                        rows, val = P, v_nsa[:, 0 if branch == "slc" else 1, j, h // GROUP, :]
                    for k, pt in enumerate((pt_hi, pt_lo)):
                        ins = mm(result(nth, 0, P, lo, hi), val, pt[0:rows, v % 2, j, lo:hi],
                                 start=(first and n == 0 and k == 0), stop=(final and n == len(jobs) - 1 and k == 1))
                ins.then_inc(s_pv, 1)
                if final:
                    pe.wait_ge(s_pv, v + 1)
                    nc.tensor.sem_inc(s_out, 1)

            for i in range(len(UNITS) + LAG_PV):
                if i < len(UNITS):
                    scores(i)
                if 0 <= i - LAG_T < len(UNITS):
                    transposes(i - LAG_T)
                if i - LAG_PV in PV_AT:
                    weighted_values(PV_AT[i - LAG_PV])

            pe.wait_ge(s_mix, HEADS * (NT // 2))
            for t in range(N_OUT):
                pe.wait_ge(s_whi, N_IN + t + 1)
                pe.wait_ge(s_wlo, N_IN + t + 1)
                if t >= 2:
                    pe.wait_ge(s_y, t - 1)
                project(N_IN + t, 0, t % 2)
                project(N_IN + t, 1, t % 2).then_inc(s_proj, 1)


_INS = ["xT", "norm_gain", "w_in", "q_norm_gain", "k_norm_cmp", "k_norm_slc", "k_norm_win",
        "cmp_k_pos", "cmp_k_w1", "cmp_k_b1", "cmp_k_w2", "cmp_v_pos", "cmp_v_w1", "cmp_v_b1", "cmp_v_w2",
        "w_out", "consts", "rotary"]


def kernel(**inputs):
    import concourse.bacc as _bacc
    from concourse.bass_utils import run_bass_kernel_spmd as _run

    nc = _bacc.Bacc("TRN2", target_bir_lowering=False, num_devices=1)
    given = {k: np.asarray(v) for k, v in inputs.items()}
    given["xT"] = given.pop("x")[0].T
    given["consts"], given["rotary"] = shape_constants()
    arrays, args = {}, []
    for name in _INS:
        a = np.ascontiguousarray(given[name])
        arrays[f"in_{name}_dram"] = a
        args.append(nc.dram_tensor(f"in_{name}_dram", a.shape, mybir.dt.from_np(a.dtype), kind="ExternalInput").ap())
    args.append(nc.dram_tensor("out_0_dram", (D, S), F32, kind="ExternalOutput").ap())
    with nc.allow_non_contiguous_dma(reason="small gains and positions"):
        build(nc, *args)
    r = _run(nc, [arrays], core_ids=[0])
    return np.ascontiguousarray(r.results[0]["out_0_dram"].T)[None]
```

```python
from contextlib import ExitStack

import numpy as np

import concourse.bass as bass
from concourse import mybir

F32 = mybir.dt.float32
F32R = mybir.dt.float32r
BF16 = mybir.dt.bfloat16
ALU = mybir.AluOpType
ACT = mybir.ActivationFunctionType
AX_X = mybir.AxisListType.X

P = 128
S = 1024
D = 1024
DH = 64
KT = D // P
NT = S // P
HALF = 512
NSA_HEADS, KV_HEADS, SB_HEADS = 8, 2, 8
GROUP = NSA_HEADS // KV_HEADS
HEADS = NSA_HEADS + SB_HEADS
N_BRANCH = 3
CMP_LEN, CMP_STRIDE = 32, 16
N_CMP = (S - CMP_LEN) // CMP_STRIDE + 1
CW = 64
WIN_TILES = 512 // P
ROPE = DH // 4
EPS = 1e-6
SCALE = 1.0 / 8.0
MASK = -1e30
PAD = -1e29

C_Q, C_KC, C_VC, C_KS, C_VS, C_KW, C_VW = 0, 512, 640, 768, 896, 1024, 1152
C_GL, C_GN, C_QB, C_KB, C_VB, C_GB = 1280, 1304, 1816, 2328, 2840, 3352
_HEAD = {"norm0": ("norm", 0, C_KS, P), "norm1": ("norm", 1, C_KW, P), "val0": ("val", 0, C_VS, P), "val1": ("val", 1, C_VW, P),
         "logit": ("logit", 0, C_GL, NSA_HEADS * N_BRANCH), "cmp0": ("cmp", 0, C_KC, P)}
for _i in range(4):
    _HEAD[f"norm{2 + _i}"] = ("norm", 2 + _i, C_Q + P * _i, P)
    _HEAD[f"gate{_i}"] = ("gate", _i, C_GN + P * _i, P)
TILES = [_HEAD[_n] for _n in ("norm0", "val0", "gate0", "norm1", "val1", "gate1", "norm2", "norm3", "gate2", "norm4",
                              "norm5", "gate3", "logit", "cmp0")]
for _i in range(4):
    TILES += [("cmp", 1, C_VC, P)] if _i == 1 else []
    TILES += [("sbq", _i, C_QB + P * _i, P), ("sbk", _i, C_KB + P * _i, P),
              ("val", 2 + _i, C_VB + P * _i, P), ("gate", 4 + _i, C_GB + P * _i, P)]
N_IN = len(TILES)
N_OUT = D // P
PREFETCH = N_IN - 6
CMP_AT = [t for t, x in enumerate(TILES) if x[0] == "cmp"][0]
HL = [(k, i) for k, i, _, _ in TILES if k in ("norm", "sbq", "sbk")]
HL_OF = {key: n for n, key in enumerate(HL)}
GATES = [(k, i) for k, i, _, _ in TILES if k == "gate"]
NORMS = [(k, i) for k, i, _, _ in TILES if k == "norm"]
VALS = [(k, i) for k, i, _, _ in TILES if k == "val"]

K_CAUSAL, K_TAIL, K_STRICT, K_CMP = 0, 128, 256, 384
K_MASKS = K_CMP + NT * CW
K_ID, K_BLOCK = K_MASKS, K_MASKS + P
K_ALL = K_BLOCK + P


ORDER = [("slc", 0), ("slc", 1), ("cmp", 1), ("win", 0), ("win", 1)]


def plan_units():
    units, pvs = [], []
    for h in range(HEADS):
        for pair in range(NT // 2):
            order = ORDER if h < NSA_HEADS else (("sb", 0), ("sb", 1))
            branches = [b for b, side in order if side == 1]
            base = len(pvs)
            for branch, side in order:
                q = 2 * pair + (side if branch != "cmp" else 0)
                k0 = max(0, q - WIN_TILES) if branch == "win" else 0
                n = 1 if branch == "cmp" else q - k0 + 1
                units.append((h, q, branch, k0, n, base + branches.index(branch)))
                if side == 1:
                    pvs.append((h, pair, branch, len(units) - 1))
    return units, pvs


UNITS, PVS = plan_units()
GROUPS, GROUP_END = [], []
for _u, (_h, _q, _b, _k0, _n, _v) in enumerate(UNITS):
    for _j in range(0, _n, 4):
        GROUPS.append((_u, _j, min(4, _n - _j)))
    GROUP_END.append(len(GROUPS))
GROUP_START = [0] + GROUP_END[:-1]
KSEQ = [("slc", 0), ("win", 0), ("slc", 1), ("win", 1)] + [("sb", h) for h in range(SB_HEADS)]
K_SLOTS = 3


def key_index(h, branch):
    return KSEQ.index((branch, h // GROUP)) if h < NSA_HEADS else KSEQ.index(("sb", h - NSA_HEADS))


K_LAST = [max(u for u, x in enumerate(UNITS) if x[2] != "cmp" and key_index(x[0], x[2]) == k) for k in range(len(KSEQ))]
HEAD_LAST = [max(u for u, x in enumerate(UNITS) if x[0] == h) for h in range(HEADS)]
OUTS = [v for v, x in enumerate(PVS) if v == len(PVS) - 1 or PVS[v + 1][0:2] != x[0:2]]
OUT_OF = {v: o for o, v in enumerate(OUTS)}
LAG_T = 3
LAG_PV = LAG_T + 2
LAG_OUT = LAG_PV
LAG_GATE = LAG_OUT - 1
LAG_HI = LAG_OUT + 1
LAG_LO = LAG_HI
PROB_COLS = 4 * S
T_BANKS, O_BANKS = 3, 1
S_BANKS = 8 - T_BANKS - O_BANKS
PARTS = {"slc": [(0, S)], "win": [(0, S)], "sb": [(0, S)], "cmp": [(0, CW), (CW, 2 * CW)]}
STAT = 8
PV_AT = {x[3]: v for v, x in enumerate(PVS)}


def place_scores():
    at, users, out = 0, [-1] * S_BANKS, []
    for u, (_, _, branch, _, n, _) in enumerate(UNITS):
        need = 1 if branch == "cmp" else -(-n * P // HALF)
        if at + need > S_BANKS:
            at = 0
        out.append((at, max(users[at:at + need])))
        users[at:at + need] = [u] * need
        at = (at + need) % S_BANKS
    return out


def place_weights():
    at, users, out = 0, [-1] * PROB_COLS, []
    for u, (_, _, branch, _, n, _) in enumerate(UNITS):
        w = n * P
        if at + w > PROB_COLS:
            at = 0
        out.append((at, max(users[at:at + w])))
        users[at:at + w] = [u] * w
        at += w
    return out


SCORES, WEIGHTS = place_scores(), place_weights()
FIRST_HIGH = min(u for u in range(len(UNITS)) if WEIGHTS[u][0] + UNITS[u][4] * P > 3 * S)
N_NSA = sum(x[2] != "sb" for x in UNITS)


def shape_constants():
    f = np.float32
    c = np.zeros((P, K_ALL), f)
    p, n = np.arange(P)[:, None], np.arange(P)[None, :]
    c[:, K_ID:K_ID + P] = p == n
    c[:, K_CAUSAL:K_CAUSAL + P] = np.where(n <= p, f(0), f(-MASK))
    c[:, K_TAIL:K_TAIL + P] = np.where(n > p, f(0), f(-MASK))
    c[:, K_STRICT:K_STRICT + P] = np.where(n < p, f(0), f(MASK))
    c[:, K_BLOCK:K_BLOCK + P] = (p // DH) == (n // DH)
    for q in range(NT):
        m = np.arange(CW)[None, :]
        ok = (m < N_CMP) & (m * CMP_STRIDE + CMP_LEN - 1 <= q * P + p)
        c[:, K_CMP + q * CW:K_CMP + (q + 1) * CW] = np.where(ok, f(0), np.where(m < N_CMP, f(-MASK), f(-PAD)))
    half = ROPE // 2
    inv = np.power(f(500000.0), -np.arange(0, ROPE, 2, dtype=f) / f(ROPE)).astype(f)
    ang = (np.arange(S, dtype=f)[:, None] * inv[None, :]).astype(f)
    cos, sin = np.cos(ang).T.astype(f), np.sin(ang).T.astype(f)
    rot = np.zeros((2, P, S), f)
    rot[0] = 1
    for b in range(0, P, DH):
        rot[0, b:b + half], rot[0, b + half:b + ROPE] = cos, cos
        rot[1, b:b + half], rot[1, b + half:b + ROPE] = -sin, sin
    return c, rot


def build(nc, xT, norm_gain, w_in, q_norm_gain, k_norm_cmp, k_norm_slc, k_norm_win,
          cmp_k_pos, cmp_k_w1, cmp_k_b1, cmp_k_w2, cmp_v_pos, cmp_v_w1, cmp_v_b1, cmp_v_w2,
          w_out, consts, rotary, outT):
    ctx = ExitStack()
    with ctx:
        early = ExitStack()

        def sb(name, shape, dt=F32, where=ctx):
            return where.enter_context(nc.sbuf_tensor(name, shape, dt))

        def sem(name):
            return ctx.enter_context(nc.semaphore(name))

        hl_dram = nc.dram_tensor("hl_scratch", [len(HL), 2, P, S], F32, kind="Internal").ap()
        gate_dram = nc.dram_tensor("gate_scratch", [len(GATES), P, S], F32, kind="Internal").ap()
        val_dram = nc.dram_tensor("val_scratch", [4, P, NT, 2, P], F32, kind="Internal").ap()

        act_hi = sb("act_hi", [P, KT, S], F32R)
        act_lo = sb("act_lo", [P, KT, S], F32R)
        w_raw = sb("w_raw", [P, 2, KT, P])
        w_hi = sb("w_hi", [P, 2, KT, P], F32R)
        w_lo = sb("w_lo", [P, 2, KT, P], F32R)
        v_nsa = sb("v_nsa", [P, 2, NT, 2, P], F32R)
        v_cmp = sb("v_cmp", [CW, 2, P], F32R)
        kc_hh = sb("kc_hh", [P, 2, CW], F32R)
        kc_ll = sb("kc_ll", [P, 2, CW], F32R)
        ident = sb("ident", [P, P])
        masks = sb("masks", [P, K_MASKS + P], BF16)
        gate_tok = sb("gate_tok", [P, NT, NSA_HEADS * N_BRANCH])
        gain_x = sb("gain_x", [P, KT])
        gains = sb("gains", [P, 4])
        bias1 = sb("bias1", [P, 2])
        neg_max = sb("neg_max", [P, STAT, 2])
        row_sum = sb("row_sum", [P, STAT, 2])
        row_inv = sb("row_inv", [P, STAT, 2])

        x_raw = sb("x_raw", [P, 2, S], where=early)
        raw2 = sb("raw2", [P, 2, S], where=early)
        normed = sb("normed", [P, S], where=early)
        square2 = sb("square2", [P, 2, S], where=early)
        inv_rms = sb("inv_rms", [P, S], where=early)
        token_inv = sb("token_inv", [P, S], where=early)
        part_hi = sb("part_hi", [P, 2, S], F32R, where=early)
        part_lo = sb("part_lo", [P, 2, S], F32R, where=early)
        v_buf = sb("v_buf", [P, NT, 2, P], F32R, where=early)
        gate_buf = sb("gate_buf", [P, S], where=early)
        swapped = sb("swapped", [P, S], where=early)
        rot = sb("rot", [P, 2, S], where=early)
        blocks_one = sb("blocks_one", [P, P], where=early)
        ones = sb("ones", [P, P], where=early)
        const_f = token_inv[:, 0:K_MASKS]
        w1 = sb("w1", [P, CMP_LEN, P], where=early)
        w2 = sb("w2", [P, 2, P], where=early)
        pos = sb("pos", [P, 2, CMP_LEN], where=early)
        x_slots = [x_raw[:, 0, :], x_raw[:, 1, :], gate_buf[:, :], inv_rms[:, :]]
        blk = x_raw[:, :, :].rearrange("p a (b c) -> p (a b) c", c=CW)
        hid = sb("hid", [P, 2, CW], where=early)
        sig = sb("sig", [P, 2, CW], where=early)
        kc_buf = sb("kc_buf", [P, 5, CW], where=early)
        kc_h = sb("kc_h", [P, CW], F32R, where=early)
        kc_l = sb("kc_l", [P, CW], F32R, where=early)
        early.close()

        q_st = sb("q_st", [P, 2, S], F32R)
        pt_hi = sb("pt_hi", [P, 2, NT, 2 * P], F32R)
        pt_lo = sb("pt_lo", [P, 2, NT, 2 * P], F32R)
        prob = sb("prob", [P, PROB_COLS])
        keep = sb("keep", [P, 2, S + 1])
        o_val = sb("o_val", [P, 2, 2 * P])
        k_hh = sb("k_hh", [P, K_SLOTS, S], F32R)
        k_ll = sb("k_ll", [P, K_SLOTS, S], F32R)
        gate_st = sb("gate_st", [P, 2, S])
        v_sb = v_nsa[:, :, :, 0, :]
        y_buf = prob[:, 0:2 * S].rearrange("p (a t) -> p a t", t=S)

        psum = ctx.enter_context(nc.psum_tensor("psum", [P, 8 * HALF], F32))
        ps_s = [psum[:, 0:2 * HALF], psum[:, 2 * HALF:4 * HALF]]
        ps_t = psum[:, 4 * HALF:6 * HALF]
        ps_o = [psum[:, 6 * HALF:7 * HALF], psum[:, 7 * HALF:8 * HALF]]
        pt_at, po_at = S_BANKS * HALF, (S_BANKS + T_BANKS) * HALF

        def score_cols(i, c, e):
            at = SCORES[i][0] * HALF
            return psum[:, at + c:at + e]

        def weight_cols(i, c, e):
            at = WEIGHTS[i][0]
            return prob[:, at + c:at + e]

        def turned(g, rows, cols):
            at = pt_at + (g % T_BANKS) * HALF
            return psum[0:rows, at:at + cols]

        def turned_at(i, g):
            h, q, branch, k0, n, v = UNITS[i]
            _, j, c = GROUPS[g]
            if branch == "cmp":
                return slice(0, CW), v % 2, slice(0, 1), slice(0, 2 * P)
            return slice(0, P), v % 2, slice(k0 + j, k0 + j + c), slice((q % 2) * P, (q % 2 + 1) * P)

        def result(o, r0, r1, c0, c1):
            at = po_at + (o % O_BANKS) * HALF
            return psum[r0:r1, at + c0:at + c1]

        s_const, s_small, s_w1 = sem("s_const"), sem("s_small"), sem("s_w1")
        s_cast, s_ones, s_zero = sem("s_cast"), sem("s_ones"), sem("s_zero")
        s_x = [sem(f"s_x{n}") for n in range(4)]
        s_xhi, s_xsq, s_xlo, s_xacc = sem("s_xhi"), sem("s_xsq"), sem("s_xlo"), sem("s_xacc")
        s_xms, s_xstd, s_tinv = sem("s_xms"), sem("s_xstd"), sem("s_tinv")
        s_w = [sem("s_wa"), sem("s_wb")]
        s_whi, s_wlo = sem("s_whi"), sem("s_wlo")
        s_proj, s_evac = sem("s_proj"), sem("s_evac")
        s_sq, s_ms, s_std, s_normed, s_swap, s_rot = (sem(n) for n in ("s_sq", "s_ms", "s_std", "s_normed", "s_swap", "s_rot"))
        s_phi, s_plo = sem("s_phi"), sem("s_plo")
        s_hl = [sem("s_hl0"), sem("s_hl1")]
        s_gsig, s_gate, s_gst = sem("s_gsig"), sem("s_gate"), sem("s_gst")
        s_vt, s_vhi, s_vlo, s_vst = (sem(n) for n in ("s_vt", "s_vhi", "s_vlo", "s_vst"))
        s_lsig, s_lt, s_ltok = sem("s_lsig"), sem("s_lt"), sem("s_ltok")
        s_blk, s_mlp, s_msig, s_hid, s_kv2 = (sem(n) for n in ("s_blk", "s_mlp", "s_msig", "s_hid", "s_kv2"))
        s_ksq, s_kms, s_kstd, s_kn, s_ksw, s_khi, s_klo, s_kst, s_vc = (
            sem(n) for n in ("s_ksq", "s_kms", "s_kstd", "s_kn", "s_ksw", "s_khi", "s_klo", "s_kst", "s_vc"))
        s_dve, s_act = sem("s_dve"), sem("s_act")
        s_ql = [sem("s_ql0"), sem("s_ql1")]
        s_kl = [sem(f"s_kl{i}") for i in range(K_SLOTS)]
        s_vl = [sem("s_vl0"), sem("s_vl1")]
        s_gl = [sem("s_gl0"), sem("s_gl1")]
        s_score, s_nmax, s_exp, s_rinv, s_keep, s_p = (sem(n) for n in ("s_score", "s_nmax", "s_exp", "s_rinv", "s_keep", "s_p"))
        s_tr, s_hi, s_lo, s_pv, s_out = (sem(n) for n in ("s_tr", "s_hi", "s_lo", "s_pv", "s_out"))
        s_olo, s_osum, s_oval, s_mhi, s_mix = sem("s_olo"), sem("s_osum"), sem("s_oval"), sem("s_mhi"), sem("s_mix")
        s_xr = [sem("s_xr0"), sem("s_xr1")]
        s_y, s_st = sem("s_y"), [sem("s_st0"), sem("s_st1")]

        def chain(s):
            n = [0]

            def link(eng, ins):
                n[0] += 1
                ins.then_inc(s, 1)
                eng.wait_ge(s, n[0])
            return link

        w_in_v = w_in.rearrange("(k p) n -> p k n", p=P)
        w_out_v = w_out.rearrange("(k p) n -> p k n", p=P)
        xT_v = xT.rearrange("(k p) t -> k p t", p=P)
        outT_v = outT.rearrange("(k p) t -> k p t", p=P)

        def w_tile(t):
            if t < N_IN:
                _, _, c, m = TILES[t]
                return w_in_v[:, :, c:c + m], m
            return w_out_v[:, :, (t - N_IN) * P:(t - N_IN + 1) * P], P

        def values(b):
            return v_nsa[:, b] if b < 2 else v_buf[:, :, :, :]

        block = ctx.enter_context(nc.Block())

        @block.sync
        def _(sp):
            def load_w(t):
                if t >= 2:
                    sp.wait_ge(s_whi, t - 1)
                    sp.wait_ge(s_wlo, t - 1)
                src, m = w_tile(t)
                sp.dma_start(w_raw[:, t % 2, :, 0:m], src).then_inc(s_w[t % 2], 16)

            load_w(0)
            sp.dma_start(gain_x[:, :], norm_gain.rearrange("(k p) -> p k", p=P)).then_inc(s_small, 16)
            for k in range(KT):
                if k >= 4:
                    sp.wait_ge(s_xlo, k - 3)
                    sp.wait_ge(s_xsq, k - 3)
                sp.dma_start(x_slots[k % 4], xT_v[k]).then_inc(s_x[k % 4], 16)
            load_w(1)
            sp.dma_start(const_f, consts[:, 0:K_MASKS]).then_inc(s_const, 16)
            sp.dma_start(rot[:, :, :], rotary.rearrange("c p t -> p c t")).then_inc(s_const, 16)
            sp.dma_start(ident[:, :], consts[:, K_ID:K_ID + P]).then_inc(s_const, 16)
            sp.dma_start(blocks_one[:, :], consts[:, K_BLOCK:K_BLOCK + P]).then_inc(s_const, 16)
            for n, g in enumerate((q_norm_gain, k_norm_slc, k_norm_win, k_norm_cmp)):
                for b in range(0, P, DH):
                    sp.dma_start(gains[b:b + DH, n:n + 1], g.rearrange("(p a) -> p a", a=1)).then_inc(s_small, 16)
            for n, (b1, w2x, px) in enumerate(((cmp_k_b1, cmp_k_w2, cmp_k_pos), (cmp_v_b1, cmp_v_w2, cmp_v_pos))):
                for b in range(0, P, DH):
                    sp.dma_start(bias1[b:b + DH, n:n + 1], b1.rearrange("(p a) -> p a", a=1)).then_inc(s_small, 16)
                    if n == 0 and b == 0:
                        sp.wait_ge(s_zero, 2)
                    sp.dma_start(w2[b:b + DH, n, b:b + DH], w2x).then_inc(s_small, 16)
                    sp.dma_start(pos[b:b + DH, n, :], px.rearrange("l d -> d l")).then_inc(s_small, 16)

            def load_w1(n):
                src = (cmp_k_w1, cmp_v_w1)[n].rearrange("(l d) j -> d l j", d=DH)
                for b in range(0, P, DH):
                    sp.dma_start(w1[b:b + DH, :, b:b + DH], src).then_inc(s_w1, 16)
            load_w1(0)
            load_w(2)

            def stacks(dst, slot, s, tile, row, order):
                for b, part in zip((0, DH), order):
                    sp.dma_start(dst[b:b + DH, slot, :].bitcast(F32), hl_dram[tile, part, row:row + DH, :]).then_inc(s, 16)

            def load_keys(k):
                branch, i = KSEQ[k]
                if k >= K_SLOTS:
                    sp.wait_ge(s_score, K_LAST[k - K_SLOTS] + 1)
                tile = HL_OF["sbk", i // 2] if branch == "sb" else HL_OF["norm", 0 if branch == "slc" else 1]
                stacks(k_hh, k % K_SLOTS, s_kl[k % K_SLOTS], tile, (i % 2) * DH, (0, 0))
                stacks(k_ll, k % K_SLOTS, s_kl[k % K_SLOTS], tile, (i % 2) * DH, (1, 1))

            def load_queries(h):
                if h >= 2:
                    sp.wait_ge(s_score, HEAD_LAST[h - 2] + 1)
                tile = HL_OF["norm", 2 + h // 2] if h < NSA_HEADS else HL_OF["sbq", (h - NSA_HEADS) // 2]
                stacks(q_st, h % 2, s_ql[h % 2], tile, (h % 2) * DH, (0, 1))

            def load_values(h):
                n = h - NSA_HEADS
                if n >= 2:
                    sp.wait_ge(s_pv, max(v for v, x in enumerate(PVS) if x[0] == h - 2) + 1)
                sp.dma_start(v_sb[:, n % 2].bitcast(F32), val_dram[n // 2, :, :, n % 2, :]).then_inc(s_vl[n % 2], 16)

            def load_gate(t):
                if t >= 2:
                    sp.wait_ge(s_mix, (NT // 2) * 2 * (t - 1))
                sp.dma_start(gate_st[:, t % 2, :], gate_dram[t]).then_inc(s_gl[t % 2], 16)

            for t, (kind, i, _, _) in enumerate(TILES):
                if t + 3 < N_IN + 2 and t != CMP_AT + 1:
                    load_w(t + 3)
                if t == CMP_AT:
                    load_w(t + 4)
                if t == CMP_AT + 2:
                    sp.wait_ge(s_mlp, 1)
                    load_w1(1)
                if kind == "norm":
                    n = NORMS.index((kind, i))
                    sp.wait_ge(s_normed, n + 1)
                    for b in range(0, P, DH):
                        sp.dma_start(swapped[b:b + 8, :], normed[b + 8:b + 16, :]).then_inc(s_swap, 16)
                        sp.dma_start(swapped[b + 8:b + 16, :], normed[b:b + 8, :]).then_inc(s_swap, 16)
                if (kind, i) in HL_OF:
                    u = HL_OF[kind, i]
                    sp.wait_ge(s_phi, u + 1)
                    sp.dma_start(hl_dram[u, 0], part_hi[:, u % 2, :].bitcast(F32)).then_inc(s_hl[u % 2], 16)
                    sp.wait_ge(s_plo, u + 1)
                    sp.dma_start(hl_dram[u, 1], part_lo[:, u % 2, :].bitcast(F32)).then_inc(s_hl[u % 2], 16)
                if kind == "gate":
                    sp.wait_ge(s_gate, GATES.index((kind, i)) + 1)
                    sp.dma_start(gate_dram[i], gate_buf[:, :]).then_inc(s_gst, 16)
                if kind == "val" and i >= 2:
                    sp.wait_ge(s_vhi, i + 1)
                    sp.wait_ge(s_vlo, i + 1)
                    sp.dma_start(val_dram[i - 2], v_buf[:, :, :, :].bitcast(F32)).then_inc(s_vst, 16)
                if t == PREFETCH:
                    sp.wait_ge(s_vc, 2)
                    sp.wait_ge(s_rot, len(NORMS))
                    for n in range(2):
                        sp.wait_ge(s_hl[n], 32 * len(range(n, len(NORMS), 2)))
                    sp.wait_ge(s_gst, 16)
                    sp.wait_ge(s_kst, 128)
                    load_queries(0)
                if PREFETCH <= t < PREFETCH + 3:
                    load_keys(t - PREFETCH)
                if t == PREFETCH + 3:
                    load_gate(0)
                if kind == "cmp" and i == 0:
                    sp.wait_ge(s_kn, 1)
                    for b in range(0, P, DH):
                        sp.dma_start(kc_buf[b:b + 8, 3, 0:N_CMP], kc_buf[b + 8:b + 16, 2, 0:N_CMP]).then_inc(s_ksw, 16)
                        sp.dma_start(kc_buf[b + 8:b + 16, 3, 0:N_CMP], kc_buf[b:b + 8, 2, 0:N_CMP]).then_inc(s_ksw, 16)
                    sp.wait_ge(s_khi, 1)
                    sp.wait_ge(s_klo, 1)
                    for g in range(KV_HEADS):
                        for b in range(0, P, DH):
                            sp.dma_start(kc_hh[b:b + DH, g, :].bitcast(F32), kc_h[g * DH:(g + 1) * DH, :].bitcast(F32)).then_inc(s_kst, 16)
                            sp.dma_start(kc_ll[b:b + DH, g, :].bitcast(F32), kc_l[g * DH:(g + 1) * DH, :].bitcast(F32)).then_inc(s_kst, 16)

            for n in range(2):
                sp.wait_ge(s_hl[n], 32 * len(range(n, len(HL), 2)))
            sp.wait_ge(s_gst, 16 * len(GATES))
            sp.wait_ge(s_vst, 16 * 4)

            for h in range(HEADS):
                if h + 1 < HEADS:
                    load_queries(h + 1)
                if h == 3:
                    load_keys(3)
                if h >= NSA_HEADS - 1 and h + 1 < HEADS:
                    if h + 1 == NSA_HEADS:
                        load_keys(4)
                    load_values(h + 1)
                    if h + 2 < HEADS:
                        load_keys(h + 2 - NSA_HEADS + 4)
                if h % 2 == 1 and h + 1 < HEADS:
                    load_gate((h + 1) // 2)

            sp.wait_ge(s_mix, HEADS * (NT // 2))
            for t in range(N_OUT):
                if t + 2 < N_OUT:
                    load_w(N_IN + t + 2)
                if t >= 2:
                    sp.wait_ge(s_st[t % 2], 16 * (t // 2))
                sp.dma_start(y_buf[:, t % 2, :], xT_v[t]).then_inc(s_xr[t % 2], 16)
                sp.wait_ge(s_y, t + 1)
                sp.dma_start(outT_v[t], y_buf[:, t % 2, :]).then_inc(s_st[t % 2], 16)
            for n in range(2):
                sp.wait_ge(s_st[n], 16 * (N_OUT // 2))

        @block.gpsimd
        def _(pool):
            nc.gpsimd.memset(ones[:, :], 1.0).then_inc(s_ones, 1)
            nc.gpsimd.memset(w2[:, :, :], 0.0).then_inc(s_zero, 1)
            nc.gpsimd.memset(w1[:, :, :], 0.0).then_inc(s_zero, 1)
            nc.gpsimd.memset(swapped[:, :], 0.0).then_inc(s_zero, 1)
            nc.gpsimd.memset(kc_buf[:, :, :], 0.0).then_inc(s_zero, 1)

            def split_lo(t):
                pool.wait_ge(s_w[t % 2], 16 * (t // 2 + 1))
                pool.wait_ge(s_whi, t + 1)
                if t >= 2:
                    pool.wait_ge(s_proj, t - 1)
                m = w_tile(t)[1]
                nc.gpsimd.tensor_tensor(w_lo[:, t % 2, :, 0:m], w_raw[:, t % 2, :, 0:m],
                                        w_hi[:, t % 2, :, 0:m].bitcast(F32), ALU.subtract).then_inc(s_wlo, 1)

            for t in range(N_IN):
                split_lo(t)
            for t in range(N_IN, N_IN + 2):
                split_lo(t)
            pool.wait_ge(s_ltok, 1)

            def weigh(i):
                h, q, branch, k0, n, v = UNITS[i]
                w = n * P
                a = weight_cols(i, 0, w)
                if branch == "sb":
                    m = i - N_NSA
                    if m < 2:
                        nc.gpsimd.memset(keep[:, m, S:S + 1], 1.0).then_inc(s_ones, 1)
                        pool.wait_ge(s_ones, m + 2)
                    pool.wait_ge(s_keep, m + 1)
                    nc.gpsimd.tensor_tensor(a, a, keep[:, m % 2, S - w + 1:S + 1], ALU.mult).then_inc(s_p, 1)
                else:
                    b = ("cmp", "slc", "win").index(branch)
                    pool.wait_ge(s_rinv, i + 1)
                    for side, (c, e) in enumerate(PARTS[branch]):
                        a = weight_cols(i, c, min(w, e))
                        ins = nc.gpsimd.tensor_scalar(a, a, row_inv[:, i % STAT, side:side + 1],
                                                      gate_tok[:, q + side, h * N_BRANCH + b:h * N_BRANCH + b + 1],
                                                      ALU.mult, ALU.mult)
                    ins.then_inc(s_p, 1)

            def gate_output(v):
                h, pair, _, _ = PVS[v]
                o, b, cols = OUT_OF[v], (h % 2) * DH, slice(pair * 2 * P, (pair + 1) * 2 * P)
                pool.wait_ge(s_osum, o + 1)
                if b:
                    pool.wait_ge(s_p, weighed[0])
                pool.wait_ge(s_gl[(h // 2) % 2], 16 * (h // 4 + 1))
                nc.gpsimd.tensor_tensor(o_val[b:b + DH, o % 2, :], o_val[b:b + DH, o % 2, :], gate_st[b:b + DH, (h // 2) % 2, cols],
                                        ALU.mult).then_inc(s_oval, 1)
                if b:
                    pool.wait_ge(s_oval, o + 1)

            def output_lo(v):
                h, pair, _, _ = PVS[v]
                o, b, cols = OUT_OF[v], (h % 2) * DH, slice(pair * 2 * P, (pair + 1) * 2 * P)
                if b:
                    pool.wait_ge(s_p, weighed[0])
                pool.wait_ge(s_mhi, o + 1)
                nc.gpsimd.tensor_tensor(act_lo[b:b + DH, h // 2, cols], o_val[b:b + DH, o % 2, :],
                                        act_hi[b:b + DH, h // 2, cols].bitcast(F32), ALU.subtract).then_inc(s_mix, 1)
                if b:
                    pool.wait_ge(s_mix, o + 1)

            weighed = [0]
            for i in range(len(UNITS) + LAG_LO):
                if i < len(UNITS):
                    weigh(i)
                    weighed[0] = i + 1
                if PV_AT.get(i - LAG_GATE) in OUT_OF:
                    gate_output(PV_AT[i - LAG_GATE])
                if PV_AT.get(i - LAG_LO) in OUT_OF:
                    output_lo(PV_AT[i - LAG_LO])
            for t in range(N_IN + 2, N_IN + N_OUT):
                split_lo(t)

        @block.scalar
        def _(act):
            link = chain(s_act)
            func = nc.scalar.activation

            def split_hi(t):
                act.wait_ge(s_w[t % 2], 16 * (t // 2 + 1))
                if t >= 2:
                    act.wait_ge(s_proj, t - 1)
                    act.wait_ge(s_wlo, t - 1)
                m = w_tile(t)[1]
                func(w_hi[:, t % 2, :, 0:m], w_raw[:, t % 2, :, 0:m], ACT.Copy).then_inc(s_whi, 1)

            split_hi(0)
            act.wait_ge(s_small, 16)
            for k in range(KT):
                act.wait_ge(s_x[k % 4], 16 * (k // 4 + 1))
                func(act_hi[:, k, :], x_slots[k % 4], ACT.Copy, scale=gain_x[:, k:k + 1]).then_inc(s_xhi, 1)
                if k >= 2:
                    act.wait_ge(s_xacc, k - 1)
                func(square2[:, k % 2, :], x_slots[k % 4], ACT.Square).then_inc(s_xsq, 1)
            split_hi(1)
            act.wait_ge(s_const, 64)
            func(masks[:, 0:K_MASKS], const_f, ACT.Copy).then_inc(s_cast, 1)
            func(masks[:, K_MASKS:K_MASKS + P], ident[:, :], ACT.Copy).then_inc(s_cast, 1)
            act.wait_ge(s_xms, 1)
            act.wait_ge(s_cast, 2)
            func(token_inv[:, :], ps_t[:, :], ACT.Sqrt, scale=1.0 / D, bias=EPS).then_inc(s_xstd, 1)

            def first(t):
                kind, i, _, m = TILES[t]
                act.wait_ge(s_evac, t + 1)
                raw, square = raw2[:, t % 2, :], square2[:, t % 2, :]
                if kind == "norm":
                    func(square, raw, ACT.Square).then_inc(s_sq, 1)
                elif kind == "gate":
                    func(square, raw, ACT.Sigmoid).then_inc(s_gsig, 1)
                elif kind == "logit":
                    func(square[0:m, :], raw[0:m, :], ACT.Sigmoid).then_inc(s_lsig, 1)

            def root(t):
                kind, i, _, _ = TILES[t]
                if kind == "norm":
                    act.wait_ge(s_ms, NORMS.index((kind, i)) + 1)
                    func(inv_rms[:, :], ps_t, ACT.Sqrt, scale=1.0 / DH, bias=EPS).then_inc(s_std, 1)

            def last(t):
                kind, i, _, _ = TILES[t]
                if (kind, i) in HL_OF:
                    u = HL_OF[kind, i]
                    if kind == "norm":
                        act.wait_ge(s_rot, NORMS.index((kind, i)) + 1)
                    if u >= 2:
                        act.wait_ge(s_hl[u % 2], 32 * (u // 2))
                    func(part_hi[:, u % 2, :], raw2[:, t % 2, :], ACT.Copy).then_inc(s_phi, 1)
                elif kind == "val":
                    act.wait_ge(s_vt, i + 1)
                    if i >= 3:
                        act.wait_ge(s_vst, 16 * (i - 2))
                    dst = values(i).rearrange("p a b c -> p (a b) c")
                    func(dst[:, :, 0:DH], ps_t.rearrange("p (a c) -> p a c", c=DH), ACT.Copy).then_inc(s_vhi, 1)
                elif kind == "cmp":
                    act.wait_ge(s_mlp, i + 1)
                    func(sig[:, i, 0:N_CMP], ps_o[i][:, 0:N_CMP], ACT.Sigmoid, bias=bias1[:, i:i + 1]).then_inc(s_msig, 1)
                    act.wait_ge(s_kv2, i + 1)
                    if i == 0:
                        link(act, func(kc_buf[:, 0, 0:N_CMP], ps_o[0][:, 64:64 + N_CMP], ACT.Copy))
                        func(kc_buf[:, 1, 0:N_CMP], kc_buf[:, 0, 0:N_CMP], ACT.Square).then_inc(s_ksq, 1)
                        act.wait_ge(s_kms, 1)
                        func(kc_buf[:, 1, 0:N_CMP], ps_o[0][:, 128:128 + N_CMP], ACT.Sqrt, scale=1.0 / DH, bias=EPS).then_inc(s_kstd, 1)
                        act.wait_ge(s_kn, 2)
                        func(kc_h[:, :], kc_buf[:, 4, :], ACT.Copy).then_inc(s_khi, 1)
                    else:
                        func(v_cmp[0:N_CMP, :, 0:DH], ps_o[1][0:N_CMP, 128:256].rearrange("p (g c) -> p g c", c=DH),
                             ACT.Copy).then_inc(s_vc, 1)

            for t in range(N_IN):
                first(t)
                if t < N_IN - 1:
                    split_hi(t + 2)
                if t >= 1:
                    last(t - 1)
                root(t)
            last(N_IN - 1)
            split_hi(N_IN + 1)
            for n in range(2):
                act.wait_ge(s_hl[n], 32 * len(range(n, len(HL), 2)))

            def weights(i):
                h, q, branch, k0, n, v = UNITS[i]
                w = n * P
                if i == FIRST_HIGH:
                    act.wait_ge(s_vst, 16 * 4)
                if WEIGHTS[i][1] >= 0:
                    act.wait_ge(s_tr, GROUP_END[WEIGHTS[i][1]])
                if branch == "sb":
                    m = i - N_NSA
                    act.wait_ge(s_score, i + 1)
                    if m >= 2:
                        act.wait_ge(s_p, i - 1)
                    func(keep[:, m % 2, S - w:S], score_cols(i, 0, w), ACT.Sigmoid, scale=-1.0)
                    func(weight_cols(i, 0, w), score_cols(i, 0, w), ACT.Sigmoid).then_inc(s_exp, 1)
                else:
                    act.wait_ge(s_nmax, i + 1)
                    for side, (c, e) in enumerate(PARTS[branch]):
                        ins = func(weight_cols(i, c, min(w, e)), score_cols(i, c, min(w, e)), ACT.Exp, scale=-1.0,
                                   bias=neg_max[:, i % STAT, side:side + 1], accum_out=row_sum[:, i % STAT, side:side + 1])
                    ins.then_inc(s_exp, 1)

            def transposed_hi(i):
                h, q, branch, k0, n, v = UNITS[i]
                if i == 0:
                    act.wait_ge(s_gate, len(GATES))
                for g in range(GROUP_START[i], GROUP_END[i]):
                    _, j, c = GROUPS[g]
                    rows, cols = (CW, 2 * P) if branch == "cmp" else (P, P)
                    act.wait_ge(s_tr, g + 1)
                    if v >= 2:
                        act.wait_ge(s_pv, v - 1)
                    at = turned_at(i, g)
                    func(pt_hi[at], turned(g, rows, c * cols).rearrange("p (a b) -> p a b", b=cols), ACT.Copy).then_inc(s_hi, 1)

            def output_copy(v):
                h, pair, _, _ = PVS[v]
                o, b = OUT_OF[v], (h % 2) * DH
                act.wait_ge(s_out, o + 1)
                if o == 0:
                    act.wait_ge(s_gst, 16 * len(GATES))
                if o >= 2:
                    act.wait_ge(s_mix, o - 1)
                func(o_val[b:b + DH, o % 2, :], result(o, DH, P, 0, 2 * P), ACT.Copy).then_inc(s_olo, 1)

            def output_hi(v):
                h, pair, _, _ = PVS[v]
                o, b = OUT_OF[v], (h % 2) * DH
                act.wait_ge(s_oval, o + 1)
                func(act_hi[b:b + DH, h // 2, pair * 2 * P:(pair + 1) * 2 * P], o_val[b:b + DH, o % 2, :], ACT.Copy).then_inc(s_mhi, 1)

            for i in range(len(UNITS) + LAG_LO):
                if 0 <= i - LAG_T < len(UNITS):
                    transposed_hi(i - LAG_T)
                if PV_AT.get(i - LAG_OUT) in OUT_OF:
                    output_copy(PV_AT[i - LAG_OUT])
                if i < len(UNITS):
                    weights(i)
                if PV_AT.get(i - LAG_HI) in OUT_OF:
                    output_hi(PV_AT[i - LAG_HI])
            for t in range(N_IN + 2, N_IN + N_OUT):
                split_hi(t)

        @block.vector
        def _(dve):
            link = chain(s_dve)
            tt, ts, stt = nc.vector.tensor_tensor, nc.vector.tensor_scalar, nc.vector.scalar_tensor_tensor
            dve.wait_ge(s_small, 16)
            for k in range(KT):
                dve.wait_ge(s_xhi, k + 1)
                stt(act_lo[:, k, :], x_slots[k % 4], gain_x[:, k:k + 1], act_hi[:, k, :].bitcast(F32),
                    ALU.mult, ALU.subtract).then_inc(s_xlo, 1)
                dve.wait_ge(s_xsq, k + 1)
                if k == 0:
                    nc.vector.tensor_copy(normed[:, :], square2[:, 0, :]).then_inc(s_xacc, 1)
                else:
                    dve.wait_ge(s_xacc, k)
                    tt(normed[:, :], normed[:, :], square2[:, k % 2, :], ALU.add).then_inc(s_xacc, 1)
            dve.wait_ge(s_small, 16 * (1 + 8 + 12))
            link(dve, ts(gains[:, 0:1], gains[:, 0:1], -SCALE, None, ALU.mult))
            dve.wait_ge(s_xstd, 1)
            nc.vector.reciprocal(token_inv[:, :], token_inv[:, :]).then_inc(s_tinv, 1)
            dve.wait_ge(s_tinv, 1)

            def evacuate(t):
                kind, _, _, m = TILES[t]
                dve.wait_ge(s_proj, t + 1)
                raw = raw2[:, t % 2, :]
                for half in range(2):
                    c = slice(half * HALF, (half + 1) * HALF)
                    if kind == "sbq":
                        ins = stt(raw[0:m, c], ps_s[t % 2][0:m, c], SCALE, token_inv[0:m, c], ALU.mult, ALU.mult)
                    else:
                        ins = tt(raw[0:m, c], ps_s[t % 2][0:m, c], token_inv[0:m, c], ALU.mult)
                ins.then_inc(s_evac, 1)
                dve.wait_ge(s_evac, t + 1)

            def normalise(t):
                kind, i, _, _ = TILES[t]
                if kind == "norm":
                    n = NORMS.index((kind, i))
                    gain = gains[:, i + 1:i + 2] if i < 2 else gains[:, 0:1]
                    dve.wait_ge(s_std, n + 1)
                    link(dve, nc.vector.reciprocal(inv_rms[:, :], inv_rms[:, :]))
                    stt(normed[:, :], raw2[:, t % 2, :], gain, inv_rms[:, :], ALU.mult, ALU.mult).then_inc(s_normed, 1)
                    dve.wait_ge(s_normed, n + 1)
                elif kind == "cmp":
                    raw = raw2[:, t % 2, :]
                    if i == 0:
                        dve.wait_ge(s_zero, 4)
                    else:
                        dve.wait_ge(s_mlp, 1)
                    tokens = raw.rearrange("p (n l) -> p l n", l=CMP_STRIDE)
                    for a in range(CMP_LEN // CMP_STRIDE):
                        ls = slice(a * CMP_STRIDE, (a + 1) * CMP_STRIDE)
                        where = pos[:, i, ls].rearrange("p (l o) -> p l o", o=1).broadcast_to([P, CMP_STRIDE, N_CMP])
                        ins = tt(blk[:, ls, 0:N_CMP], tokens[:, :, a:a + N_CMP], where, ALU.add)
                    ins.then_inc(s_blk, 1)

            def finish(t):
                kind, i, _, m = TILES[t]
                raw, square = raw2[:, t % 2, :], square2[:, t % 2, :]
                if kind == "norm":
                    n = NORMS.index((kind, i))
                    link(dve, tt(raw, normed[:, :], rot[:, 0, :], ALU.mult))
                    dve.wait_ge(s_swap, 64 * (n + 1))
                    link(dve, tt(swapped[:, :], swapped[:, :], rot[:, 1, :], ALU.mult))
                    tt(raw, raw, swapped[:, :], ALU.add).then_inc(s_rot, 1)
                    dve.wait_ge(s_rot, n + 1)
                if (kind, i) in HL_OF:
                    u = HL_OF[kind, i]
                    dve.wait_ge(s_phi, u + 1)
                    tt(part_lo[:, u % 2, :], raw, part_hi[:, u % 2, :].bitcast(F32), ALU.subtract).then_inc(s_plo, 1)
                    dve.wait_ge(s_plo, u + 1)
                elif kind == "gate":
                    n = GATES.index((kind, i))
                    dve.wait_ge(s_gsig, n + 1)
                    if n >= 1:
                        dve.wait_ge(s_gst, 16 * n)
                    tt(gate_buf[:, :], raw, square, ALU.mult).then_inc(s_gate, 1)
                    dve.wait_ge(s_gate, n + 1)
                elif kind == "logit":
                    dve.wait_ge(s_lt, 1)
                    nc.vector.tensor_copy(gate_tok[:, :, :], ps_t[:, 0:NT * m].rearrange("p (a b) -> p a b", b=m)).then_inc(s_ltok, 1)
                elif kind == "val":
                    dve.wait_ge(s_vhi, i + 1)
                    dst = values(i).rearrange("p a b c -> p (a b) c")
                    tt(dst[:, :, DH:P], ps_t.rearrange("p (a c) -> p a c", c=DH), dst[:, :, 0:DH].bitcast(F32),
                       ALU.subtract).then_inc(s_vlo, 1)
                    dve.wait_ge(s_vlo, i + 1)
                elif kind == "cmp":
                    dve.wait_ge(s_msig, i + 1)
                    stt(hid[:, i, 0:N_CMP], ps_o[i][:, 0:N_CMP], bias1[:, i:i + 1], sig[:, i, 0:N_CMP],
                        ALU.add, ALU.mult).then_inc(s_hid, 1)
                    if i == 0:
                        dve.wait_ge(s_kstd, 1)
                        link(dve, nc.vector.reciprocal(kc_buf[:, 1, 0:N_CMP], kc_buf[:, 1, 0:N_CMP]))
                        stt(kc_buf[:, 2, 0:N_CMP], kc_buf[:, 0, 0:N_CMP], gains[:, 3:4], kc_buf[:, 1, 0:N_CMP],
                            ALU.mult, ALU.mult).then_inc(s_kn, 1)
                        dve.wait_ge(s_kn, 1)
                        ends = rot[:, :, CMP_LEN - 1:S:CMP_STRIDE]
                        dve.wait_ge(s_ksw, 64)
                        link(dve, tt(kc_buf[:, 0, 0:N_CMP], kc_buf[:, 2, 0:N_CMP], ends[:, 0, :], ALU.mult))
                        link(dve, tt(kc_buf[:, 3, 0:N_CMP], kc_buf[:, 3, 0:N_CMP], ends[:, 1, :], ALU.mult))
                        tt(kc_buf[:, 4, 0:N_CMP], kc_buf[:, 0, 0:N_CMP], kc_buf[:, 3, 0:N_CMP], ALU.add).then_inc(s_kn, 1)
                        dve.wait_ge(s_kn, 2)
                        dve.wait_ge(s_khi, 1)
                        tt(kc_l[:, :], kc_buf[:, 4, :], kc_h[:, :].bitcast(F32), ALU.subtract).then_inc(s_klo, 1)
                        link(dve, nc.vector.memset(v_cmp[:, :, :].bitcast(mybir.dt.uint32), 0))
                    else:
                        dve.wait_ge(s_vc, 1)
                        tt(v_cmp[0:N_CMP, :, DH:P], ps_o[1][0:N_CMP, 128:256].rearrange("p (g c) -> p g c", c=DH),
                           v_cmp[0:N_CMP, :, 0:DH].bitcast(F32), ALU.subtract).then_inc(s_vc, 1)

            for t in range(N_IN):
                evacuate(t)
                if t >= 1:
                    finish(t - 1)
                normalise(t)
            finish(N_IN - 1)

            def maximum(i):
                h, q, branch, k0, n, v = UNITS[i]
                w = n * P
                sides = len(PARTS[branch])
                dve.wait_ge(s_score, i + 1)
                if i >= STAT:
                    dve.wait_ge(s_exp, i - STAT + 1)
                nc.vector.tensor_reduce(neg_max[:, i % STAT, 0:sides], score_cols(i, 0, w).rearrange("p (a b) -> p a b", a=sides),
                                        AX_X, ALU.min).then_inc(s_nmax, 1)

            def row_factor(i):
                h, q, branch, k0, n, v = UNITS[i]
                sides = len(PARTS[branch])
                dve.wait_ge(s_exp, i + 1)
                if branch == "sb":
                    w, m = n * P, i - N_NSA
                    row = keep[:, m % 2, S - w:S][:, ::-1]
                    nc.vector.tensor_tensor_scan(row, row, row, 1.0, ALU.mult, ALU.bypass).then_inc(s_keep, 1)
                    return
                if i >= STAT:
                    dve.wait_ge(s_p, i - STAT + 1)
                nc.vector.reciprocal(row_inv[:, i % STAT, 0:sides], row_sum[:, i % STAT, 0:sides]).then_inc(s_rinv, 1)

            def transposed_lo(i):
                h, q, branch, k0, n, v = UNITS[i]
                for g in range(GROUP_START[i], GROUP_END[i]):
                    _, j, c = GROUPS[g]
                    rows, cols = (CW, 2 * P) if branch == "cmp" else (P, P)
                    at = turned_at(i, g)
                    dve.wait_ge(s_hi, g + 1)
                    tt(pt_lo[at], turned(g, rows, c * cols).rearrange("p (a b) -> p a b", b=cols),
                       pt_hi[at].bitcast(F32), ALU.subtract).then_inc(s_lo, 1)

            def output(v):
                h, pair, _, _ = PVS[v]
                o, b = OUT_OF[v], (h % 2) * DH
                dve.wait_ge(s_olo, o + 1)
                tt(o_val[b:b + DH, o % 2, :], result(o, 0, DH, 0, 2 * P), o_val[b:b + DH, o % 2, :], ALU.add).then_inc(s_osum, 1)

            for i in range(len(UNITS) + LAG_LO):
                if i < N_NSA:
                    maximum(i)
                if 1 <= i <= len(UNITS):
                    row_factor(i - 1)
                if 0 <= i - LAG_T < len(UNITS):
                    transposed_lo(i - LAG_T)
                if PV_AT.get(i - LAG_OUT) in OUT_OF:
                    output(PV_AT[i - LAG_OUT])
            for t in range(N_OUT):
                dve.wait_ge(s_xr[t % 2], 16 * (t // 2 + 1))
                dve.wait_ge(s_proj, N_IN + t + 1)
                for half in range(2):
                    c = slice(half * HALF, (half + 1) * HALF)
                    ins = tt(y_buf[:, t % 2, c], ps_s[t % 2][:, c], y_buf[:, t % 2, c], ALU.add)
                ins.then_inc(s_y, 1)

        @block.tensor
        def _(pe):
            mm = nc.tensor.matmul

            def project(t, half, slot):
                m = w_tile(t)[1]
                c = slice(half * HALF, (half + 1) * HALF)
                for k in range(KT):
                    if t == 0:
                        pe.wait_ge(s_xhi, k + 1)
                        pe.wait_ge(s_xlo, k + 1)
                    for n, (w, a) in enumerate(((w_hi, act_hi), (w_hi, act_lo), (w_lo, act_hi))):
                        ins = mm(ps_s[slot][0:m, c], w[:, t % 2, k, 0:m], a[:, k, c],
                                 start=(k == 0 and n == 0), stop=(k == KT - 1 and n == 2))
                return ins

            def side_work(t):
                kind, i, _, m = TILES[t]
                if kind in ("norm", "val", "logit"):
                    before = [x for x in TILES[:t] if x[0] in ("norm", "val", "logit")]
                    if not before:
                        pe.wait_ge(s_xstd, 1)
                    elif before[-1][0] == "norm":
                        pe.wait_ge(s_std, NORMS.index(before[-1][0:2]) + 1)
                    elif before[-1][0] == "val":
                        pe.wait_ge(s_vlo, before[-1][1] + 1)
                    else:
                        pe.wait_ge(s_ltok, 1)
                if kind == "norm":
                    pe.wait_ge(s_sq, NORMS.index((kind, i)) + 1)
                    for half in range(2):
                        c = slice(half * HALF, (half + 1) * HALF)
                        ins = mm(ps_t[:, c], blocks_one[:, :], square2[:, t % 2, c], start=True, stop=True)
                    ins.then_inc(s_ms, 1)
                elif kind == "val":
                    pe.wait_ge(s_evac, t + 1)
                    for j in range(NT):
                        ins = nc.tensor.transpose(ps_t[:, j * P:(j + 1) * P], raw2[:, t % 2, j * P:(j + 1) * P], ident[:, :])
                    ins.then_inc(s_vt, 1)
                elif kind == "logit":
                    pe.wait_ge(s_lsig, 1)
                    for j in range(NT):
                        ins = nc.tensor.transpose(ps_t[:, j * m:(j + 1) * m], square2[0:m, t % 2, j * P:(j + 1) * P], ident[0:m, 0:m])
                    ins.then_inc(s_lt, 1)
                elif kind == "cmp":
                    pe.wait_ge(s_w1, 32 * (i + 1))
                    pe.wait_ge(s_blk, i + 1)
                    for l in range(CMP_LEN):
                        ins = mm(ps_o[i][:, 0:N_CMP], w1[:, l, :], blk[:, l, 0:N_CMP], start=(l == 0), stop=(l == CMP_LEN - 1))
                    ins.then_inc(s_mlp, 1)

            def second_layer(t):
                kind, i, _, _ = TILES[t]
                if kind == "cmp":
                    pe.wait_ge(s_hid, i + 1)
                    if i == 0:
                        mm(ps_o[0][:, 64:64 + N_CMP], w2[:, 0, :], hid[:, 0, 0:N_CMP], start=True, stop=True).then_inc(s_kv2, 1)
                    else:
                        mm(ps_o[1][0:N_CMP, 128:256], hid[:, 1, 0:N_CMP], w2[:, 1, :], start=True, stop=True).then_inc(s_kv2, 1)

            def compressed_norm(t):
                if TILES[t][0:2] == ("cmp", 0):
                    pe.wait_ge(s_ksq, 1)
                    mm(ps_o[0][:, 128:128 + N_CMP], blocks_one[:, :], kc_buf[:, 1, 0:N_CMP], start=True, stop=True).then_inc(s_kms, 1)

            for t in range(N_IN):
                pe.wait_ge(s_whi, t + 1)
                pe.wait_ge(s_wlo, t + 1)
                if t >= 2:
                    pe.wait_ge(s_evac, t - 1)
                project(t, 0, t % 2)
                if t == 0:
                    pe.wait_ge(s_ones, 1)
                    pe.wait_ge(s_xacc, KT)
                    for half in range(2):
                        c = slice(half * HALF, (half + 1) * HALF)
                        ins = mm(ps_t[:, c], ones[:, :], normed[:, c], start=True, stop=True)
                    ins.then_inc(s_xms, 1)
                else:
                    if t >= 2:
                        second_layer(t - 2)
                    side_work(t - 1)
                project(t, 1, t % 2).then_inc(s_proj, 1)
                if t >= 2:
                    compressed_norm(t - 2)
            side_work(N_IN - 1)
            pe.wait_ge(s_evac, N_IN)
            pe.wait_ge(s_kst, 128)
            pe.wait_ge(s_cast, 2)
            pe.wait_ge(s_vc, 2)
            id_b = masks[:, K_MASKS:K_MASKS + P]

            def scores(i):
                h, q, branch, k0, n, v = UNITS[i]
                if SCORES[i][1] >= 0:
                    pe.wait_ge(s_exp, SCORES[i][1] + 1)
                pe.wait_ge(s_ql[h % 2], 32 * (h // 2 + 1))
                if branch == "cmp":
                    hh, ll = kc_hh[:, h // GROUP, :], kc_ll[:, h // GROUP, :]
                    for side, (c, e) in enumerate(PARTS[branch]):
                        qs, col = q_st[:, h % 2, (q + side) * P:(q + side + 1) * P], K_CMP + (q + side) * CW
                        mm(score_cols(i, c, e), qs, hh, start=True, stop=False)
                        mm(score_cols(i, c, e), id_b, masks[:, col:col + CW], start=False, stop=False)
                        ins = mm(score_cols(i, c, e), qs, ll, start=False, stop=True)
                    ins.then_inc(s_score, 1)
                    return
                else:
                    k = key_index(h, branch)
                    pe.wait_ge(s_kl[k % K_SLOTS], 64 * (k // K_SLOTS + 1))
                    hh, ll, w = k_hh[:, k % K_SLOTS, k0 * P:(k0 + n) * P], k_ll[:, k % K_SLOTS, k0 * P:(k0 + n) * P], n * P
                    masked = {w - P: (K_STRICT if branch == "sb" else K_CAUSAL, P)}
                    if branch == "win" and q >= WIN_TILES:
                        masked[0] = (K_TAIL, P)
                qs = q_st[:, h % 2, q * P:(q + 1) * P]
                for c in range(0, w, HALF):
                    e = min(w, c + HALF)
                    mm(score_cols(i, c, e), qs, hh[:, c:e], start=True, stop=False)
                    for at, (col, mw) in masked.items():
                        if c <= at < e:
                            mm(score_cols(i, at, at + mw), id_b, masks[:, col:col + mw], start=False, stop=False)
                    ins = mm(score_cols(i, c, e), qs, ll[:, c:e], start=False, stop=True)
                ins.then_inc(s_score, 1)

            def transposes(i):
                h, q, branch, k0, n, v = UNITS[i]
                pe.wait_ge(s_p, i + 1)
                if i == 0:
                    pe.wait_ge(s_vlo, len(VALS))
                for g in range(GROUP_START[i], GROUP_END[i]):
                    _, j, c = GROUPS[g]
                    if g >= T_BANKS:
                        pe.wait_ge(s_lo, g - T_BANKS + 1)
                    jobs = PARTS["cmp"] if branch == "cmp" else [((j + a) * P, (j + a + 1) * P) for a in range(c)]
                    for a, (k, e) in enumerate(jobs):
                        to = turned(g, e - k, 4 * P)[:, a * P:(a + 1) * P]
                        ins = nc.tensor.transpose(to, weight_cols(i, k, e), ident[:, :])
                    ins.then_inc(s_tr, 1)

            def weighted_values(v):
                h, pair, branch, last = PVS[v]
                nth = len([x for x in OUTS if x < v])
                pe.wait_ge(s_lo, GROUP_END[last])
                first = v == 0 or PVS[v - 1][0:2] != PVS[v][0:2]
                if first and nth >= O_BANKS:
                    pe.wait_ge(s_osum, nth - O_BANKS + 1)
                if branch == "cmp":
                    jobs = [(0, 0, 2 * P)]
                else:
                    k0 = [min(u[3] for u in UNITS if u[5] == v and u[1] % 2 == side) for side in range(2)]
                    jobs = []
                    for j in range(min(k0), 2 * pair + 2):
                        lo = 0 if j <= 2 * pair else P
                        hi = 2 * P if j >= k0[1] else P
                        jobs.append((j, lo, hi))
                if branch == "sb":
                    n = h - NSA_HEADS
                    pe.wait_ge(s_vl[n % 2], 16 * (n // 2 + 1))
                final = v in OUT_OF
                for n, (j, lo, hi) in enumerate(jobs):
                    if branch == "cmp":
                        rows, val = CW, v_cmp[:, h // GROUP, :]
                    elif branch == "sb":
                        rows, val = P, v_sb[:, (h - NSA_HEADS) % 2, j, :]
                    else:
                        rows, val = P, v_nsa[:, 0 if branch == "slc" else 1, j, h // GROUP, :]
                    for k, pt in enumerate((pt_hi, pt_lo)):
                        ins = mm(result(nth, 0, P, lo, hi), val, pt[0:rows, v % 2, j, lo:hi],
                                 start=(first and n == 0 and k == 0), stop=(final and n == len(jobs) - 1 and k == 1))
                ins.then_inc(s_pv, 1)
                if final:
                    pe.wait_ge(s_pv, v + 1)
                    nc.tensor.sem_inc(s_out, 1)

            for i in range(len(UNITS) + LAG_PV):
                if i < len(UNITS):
                    scores(i)
                if 0 <= i - LAG_T < len(UNITS):
                    transposes(i - LAG_T)
                if i - LAG_PV in PV_AT:
                    weighted_values(PV_AT[i - LAG_PV])

            pe.wait_ge(s_mix, HEADS * (NT // 2))
            for t in range(N_OUT):
                pe.wait_ge(s_whi, N_IN + t + 1)
                pe.wait_ge(s_wlo, N_IN + t + 1)
                if t >= 2:
                    pe.wait_ge(s_y, t - 1)
                project(N_IN + t, 0, t % 2)
                project(N_IN + t, 1, t % 2).then_inc(s_proj, 1)


_INS = ["xT", "norm_gain", "w_in", "q_norm_gain", "k_norm_cmp", "k_norm_slc", "k_norm_win",
        "cmp_k_pos", "cmp_k_w1", "cmp_k_b1", "cmp_k_w2", "cmp_v_pos", "cmp_v_w1", "cmp_v_b1", "cmp_v_w2",
        "w_out", "consts", "rotary"]


def kernel(**inputs):
    import concourse.bacc as _bacc
    from concourse.bass_utils import run_bass_kernel_spmd as _run

    nc = _bacc.Bacc("TRN2", target_bir_lowering=False, num_devices=1)
    given = {k: np.asarray(v) for k, v in inputs.items()}
    given["xT"] = given.pop("x")[0].T
    given["consts"], given["rotary"] = shape_constants()
    arrays, args = {}, []
    for name in _INS:
        a = np.ascontiguousarray(given[name])
        arrays[f"in_{name}_dram"] = a
        args.append(nc.dram_tensor(f"in_{name}_dram", a.shape, mybir.dt.from_np(a.dtype), kind="ExternalInput").ap())
    args.append(nc.dram_tensor("out_0_dram", (D, S), F32, kind="ExternalOutput").ap())
    with nc.allow_non_contiguous_dma(reason="small gains and positions"):
        build(nc, *args)
    r = _run(nc, [arrays], core_ids=[0])
    return np.ascontiguousarray(r.results[0]["out_0_dram"].T)[None]
```
